# Optimizing a Trainium2 kernel written in Bass

```python
import jax, jax.numpy as jnp
from jax import lax
import numpy as np

D_MODEL = 1024
BATCH = 1
SEQ = 512
DEPTH = 1

ATTN_GROUPS = ((128, 1), (512, 4), (2048, 16))
ATTN_HEADS_PER_GROUP = 8
ATTN_HEAD_DIM = 64
ATTN_BLOCK = 128
N_ATTN_HEADS = len(ATTN_GROUPS) * ATTN_HEADS_PER_GROUP
ATTN_QKV_WIDTH = 3 * N_ATTN_HEADS * ATTN_HEAD_DIM
ATTN_OUT = ATTN_HEADS_PER_GROUP * ATTN_HEAD_DIM

GLA_HEADS = 4
GLA_DK = D_MODEL // 2
GLA_DV = D_MODEL
GLA_HK = GLA_DK // GLA_HEADS
GLA_HV = GLA_DV // GLA_HEADS
GLA_GATE_RANK = 16
GLA_TAU = 16.0
GLA_CHUNK = 64

D_FF = 4 * D_MODEL

N_BRANCHES = 2
EPS = 1e-6

_IN_SIZES = (ATTN_QKV_WIDTH, GLA_DK, GLA_DK, GLA_DV, GLA_DV, GLA_GATE_RANK, N_BRANCHES * D_MODEL)
D_IN = sum(_IN_SIZES)
_IN_OFFSETS = tuple(int(v) for v in np.cumsum(_IN_SIZES)[:-1])


def rms_norm(x, g):
    xf = x.astype(jnp.float32)
    y = xf * lax.rsqrt(jnp.mean(jnp.square(xf), axis=-1, keepdims=True) + EPS)
    return (y * g.astype(jnp.float32)).astype(x.dtype)

def _dilated_group(q, k, v, window, dilation):
    b, s, h, e = q.shape
    n_back = window // dilation
    blk = ATTN_BLOCK
    assert n_back <= blk
    seg = dilation * blk
    s_pad = -(-s // seg) * seg
    L = s_pad // dilation
    nb = L // blk

    def to_blocks(t):
        t = jnp.pad(t, ((0, 0), (0, s_pad - s), (0, 0), (0, 0)))
        t = t.reshape(b, L, dilation, h, e).transpose(0, 2, 3, 1, 4)
        return t.reshape(b, dilation, h, nb, blk, e)

    def with_prev(t):
        prev = jnp.pad(t[:, :, :, :-1], ((0, 0), (0, 0), (0, 0), (1, 0), (0, 0), (0, 0)))
        return jnp.concatenate([prev, t], axis=4)

    qb, kb, vb = to_blocks(q), to_blocks(k), to_blocks(v)
    kw, vw = with_prev(kb), with_prev(vb)
    scores = jnp.einsum('bdhnqe,bdhnke->bdhnqk', qb, kw).astype(jnp.float32) * (e ** -0.5)
    qi = jnp.arange(blk)[:, None]
    ki = jnp.arange(2 * blk)[None, :]
    dist = blk + qi - ki
    first = (jnp.arange(nb) == 0)[:, None, None]
    valid = (dist >= 0) & (dist <= n_back) & ~(first & (ki < blk))
    scores = jnp.where(valid, scores, -jnp.inf)
    mx = jnp.max(scores, axis=-1, keepdims=True)
    p = jnp.exp(scores - mx)
    den = jnp.sum(p, axis=-1, keepdims=True)
    o = jnp.einsum('bdhnqk,bdhnke->bdhnqe', p, vw.astype(jnp.float32)) / den
    lse = (mx + jnp.log(den))[..., 0]
    o = o.reshape(b, dilation, h, L, e).transpose(0, 3, 1, 2, 4).reshape(b, s_pad, h, e)[:, :s]
    lse = lse.reshape(b, dilation, h, L).transpose(0, 3, 1, 2).reshape(b, s_pad, h)[:, :s]
    return o, lse

def dilated_attention(q, k, v, gq, gk):
    b, s = q.shape[:2]
    q = rms_norm(q, gq)
    k = rms_norm(k, gk)
    outs, lses = [], []
    for gi, (window, dilation) in enumerate(ATTN_GROUPS):
        sl = slice(gi * ATTN_HEADS_PER_GROUP, (gi + 1) * ATTN_HEADS_PER_GROUP)
        o, l = _dilated_group(q[:, :, sl], k[:, :, sl], v[:, :, sl], window, dilation)
        outs.append(o)
        lses.append(l)
    wts = jax.nn.softmax(jnp.stack(lses, axis=0), axis=0)
    o = jnp.sum(wts[..., None] * jnp.stack(outs, axis=0), axis=0)
    return o.reshape(b, s, ATTN_OUT).astype(v.dtype)

def gated_linear_attention(q, k, v, log_a):
    b, s, h, dk = q.shape
    dv = v.shape[-1]
    c = GLA_CHUNK
    n = s // c

    def chunks(t):
        return t.reshape(b, n, c, h, t.shape[-1]).transpose(1, 0, 3, 2, 4).astype(jnp.float32)

    qc = chunks(q) * (dk ** -0.5)
    kc, vc, ac = chunks(k), chunks(v), chunks(log_a)
    causal = jnp.tril(jnp.ones((c, c), dtype=bool))[:, :, None]

    def step(state, inp):
        qt, kt, vt, at = inp
        bcum = jnp.cumsum(at, axis=2)
        o_inter = jnp.einsum('bhtk,bhkv->bhtv', qt * jnp.exp(bcum), state)
        diff = bcum[:, :, :, None, :] - bcum[:, :, None, :, :]
        decay = jnp.exp(jnp.where(causal, diff, -jnp.inf))
        attn = jnp.einsum('bhtk,bhsk,bhtsk->bhts', qt, kt, decay)
        o_intra = jnp.einsum('bhts,bhsv->bhtv', attn, vt)
        blast = bcum[:, :, -1:, :]
        state = (jnp.exp(blast[:, :, 0, :])[..., None] * state
                 + jnp.einsum('bhsk,bhsv->bhkv', kt * jnp.exp(blast - bcum), vt))
        return state, o_inter + o_intra

    state0 = jnp.zeros((b, h, dk, dv), jnp.float32)
    _, o = lax.scan(step, state0, (qc, kc, vc, ac))
    return o.transpose(1, 0, 3, 2, 4).reshape(b, s, h, dv).astype(v.dtype)

def first_inputs(seed: int = 0) -> dict:
    key = jax.random.key(seed)
    ks = jax.random.split(key, 16)
    f32 = jnp.float32

    def dense(k, fan_in, fan_out):
        return jax.random.normal(k, (DEPTH, fan_in, fan_out), f32) * fan_in ** -0.5

    def gain(k, n):
        return 1.0 + 0.02 * jax.random.normal(k, (DEPTH, n), f32)

    return {
        'x': jax.random.normal(ks[0], (BATCH, SEQ, D_MODEL), f32),
        'norm1_g': gain(ks[1], D_MODEL),
        'w_in': dense(ks[2], D_MODEL, D_IN),
        'attn_q_norm_g': gain(ks[3], ATTN_HEAD_DIM),
        'attn_k_norm_g': gain(ks[4], ATTN_HEAD_DIM),
        'gla_gate_up': dense(ks[5], GLA_GATE_RANK, GLA_DK),
        'gla_gate_bias': 0.1 * jax.random.normal(ks[6], (DEPTH, GLA_DK), f32),
        'gla_out_norm_g': gain(ks[7], GLA_HV),
        'branch_gate_bias': 0.1 * jax.random.normal(ks[8], (DEPTH, N_BRANCHES * D_MODEL), f32),
        'w_attn_branch': dense(ks[9], ATTN_OUT, D_MODEL),
        'w_gla_branch': dense(ks[10], GLA_DV, D_MODEL),
        'w_out': dense(ks[11], D_MODEL, D_MODEL),
        'norm2_g': gain(ks[12], D_MODEL),
        'w_ff_up': dense(ks[13], D_MODEL, D_FF),
        'w_ff_down': dense(ks[14], D_FF, D_MODEL),
    }

def first_block(x, norm1_g, w_in, attn_q_norm_g, attn_k_norm_g, gla_gate_up, gla_gate_bias,
              gla_out_norm_g, branch_gate_bias, w_attn_branch, w_gla_branch, w_out,
              norm2_g, w_ff_up, w_ff_down):
    b, s, _ = x.shape
    for l in range(DEPTH):
        h = rms_norm(x, norm1_g[l])
        proj = jnp.einsum('bsd,de->bse', h, w_in[l])
        p_attn, p_q, p_k, p_v, p_r, p_a, p_gate = jnp.split(proj, _IN_OFFSETS, axis=-1)

        qkv = p_attn.reshape(b, s, 3, N_ATTN_HEADS, ATTN_HEAD_DIM)
        o_attn = dilated_attention(qkv[:, :, 0], qkv[:, :, 1], qkv[:, :, 2],
                                   attn_q_norm_g[l], attn_k_norm_g[l])

        gate_logits = (p_a @ gla_gate_up[l] + gla_gate_bias[l]).astype(jnp.float32)
        log_a = jax.nn.log_sigmoid(gate_logits) / GLA_TAU
        o_gla = gated_linear_attention(
            p_q.reshape(b, s, GLA_HEADS, GLA_HK),
            p_k.reshape(b, s, GLA_HEADS, GLA_HK),
            p_v.reshape(b, s, GLA_HEADS, GLA_HV),
            log_a.reshape(b, s, GLA_HEADS, GLA_HK))
        o_gla = rms_norm(o_gla, gla_out_norm_g[l]).reshape(b, s, GLA_DV) * jax.nn.silu(p_r)

        gates = jax.nn.sigmoid(p_gate + branch_gate_bias[l]).reshape(b, s, N_BRANCHES, D_MODEL)
        mixed = (gates[:, :, 0] * (o_attn @ w_attn_branch[l])
                 + gates[:, :, 1] * (o_gla @ w_gla_branch[l]))
        x = x + mixed @ w_out[l]

        h2 = rms_norm(x, norm2_g[l])
        x = x + jnp.square(jax.nn.relu(h2 @ w_ff_up[l])) @ w_ff_down[l]
    return x


DEPTH_2 = 2

HEAD_DIM = 64
A_Q_HEADS = 8
A_KV_HEADS = 2
A_GROUP = A_Q_HEADS // A_KV_HEADS
A_WINDOW = 128
A_BLOCK = 128
B_HEADS = 8
GRID_W = 64
NA_KH = 8
NA_KW = 16
RET_HEADS = 8
RET_DK = D_MODEL // RET_HEADS
RET_DV = 2 * D_MODEL // RET_HEADS
RET_CHUNK = 128
D_FF_2 = 4 * D_MODEL
N_EVEN = (DEPTH_2 + 1) // 2
N_ODD = DEPTH_2 // 2
EVEN_SPLITS = (A_Q_HEADS * HEAD_DIM, A_KV_HEADS * HEAD_DIM, A_KV_HEADS * HEAD_DIM,
               B_HEADS * HEAD_DIM, B_HEADS * HEAD_DIM, B_HEADS * HEAD_DIM)
EVEN_IN = sum(EVEN_SPLITS)
EVEN_MIX = (A_Q_HEADS + B_HEADS) * HEAD_DIM
ODD_SPLITS = (RET_HEADS * RET_DK, RET_HEADS * RET_DK, RET_HEADS * RET_DV, RET_HEADS * RET_DV)
ODD_IN = sum(ODD_SPLITS)
ODD_MIX = RET_HEADS * RET_DV
RMS_EPS = 1e-6
GN_EPS = 1e-5


def _split(t, sizes):
    idx = np.cumsum(sizes)[:-1].tolist()
    return jnp.split(t, idx, axis=-1)

def _rmsnorm(x, g):
    xf = x.astype(jnp.float32)
    y = xf * lax.rsqrt(jnp.mean(xf * xf, axis=-1, keepdims=True) + RMS_EPS)
    return (y * g.astype(jnp.float32)).astype(x.dtype)

def _alibi_slopes(n):
    return 2.0 ** (-(8.0 / n) * (jnp.arange(n, dtype=jnp.float32) + 1.0))

def _window_gqa(q, k, v, sink):
    B, S = q.shape[0], q.shape[1]
    nb = S // A_BLOCK
    qb = q.reshape(B, nb, A_BLOCK, A_KV_HEADS, A_GROUP, HEAD_DIM)
    pad = ((0, 0), (A_BLOCK, A_BLOCK), (0, 0), (0, 0))
    kp = jnp.pad(k, pad).reshape(B, nb + 2, A_BLOCK, A_KV_HEADS, HEAD_DIM)
    vp = jnp.pad(v, pad).reshape(B, nb + 2, A_BLOCK, A_KV_HEADS, HEAD_DIM)
    kb = jnp.concatenate([kp[:, :-2], kp[:, 1:-1], kp[:, 2:]], axis=2)
    vb = jnp.concatenate([vp[:, :-2], vp[:, 1:-1], vp[:, 2:]], axis=2)
    s = jnp.einsum('bnqhgd,bnkhd->bnhgqk', qb, kb).astype(jnp.float32) * (HEAD_DIM ** -0.5)
    qi = jnp.arange(A_BLOCK)[:, None]
    kj = jnp.arange(3 * A_BLOCK)[None, :]
    rel = kj - A_BLOCK - qi
    kpos = jnp.arange(nb)[:, None, None] * A_BLOCK + kj[None] - A_BLOCK
    valid = (jnp.abs(rel) <= A_WINDOW)[None] & (kpos >= 0) & (kpos < S)
    slopes = _alibi_slopes(A_Q_HEADS).reshape(A_KV_HEADS, A_GROUP, 1, 1)
    s = s - slopes * jnp.abs(rel).astype(jnp.float32)
    s = jnp.where(valid[None, :, None, None], s, -jnp.inf)
    sk = sink.astype(jnp.float32).reshape(A_KV_HEADS, A_GROUP)[None, None, :, :, None, None]
    m = jnp.maximum(jnp.max(s, axis=-1, keepdims=True), sk)
    p = jnp.exp(s - m)
    p = p / (jnp.sum(p, axis=-1, keepdims=True) + jnp.exp(sk - m))
    o = jnp.einsum('bnhgqk,bnkhd->bnqhgd', p.astype(v.dtype), vb)
    return o.reshape(B, S, A_Q_HEADS * HEAD_DIM)

def _neighbourhood_attn(q, k, v, rpb):
    B, S = q.shape[0], q.shape[1]
    rows = S // GRID_W
    kh = min(NA_KH, rows)
    kw = NA_KW
    qg = q.reshape(B, rows, GRID_W, B_HEADS, HEAD_DIM)
    kg = k.reshape(B, rows, GRID_W, B_HEADS, HEAD_DIM)
    vg = v.reshape(B, rows, GRID_W, B_HEADS, HEAD_DIM)
    qc = jnp.arange(GRID_W)
    cstart = jnp.clip(qc - kw // 2, 0, GRID_W - kw)
    kc = jnp.arange(GRID_W)
    col_valid = (kc[None, :] >= cstart[:, None]) & (kc[None, :] < cstart[:, None] + kw)
    col_idx = jnp.clip(kc[None, :] - qc[:, None] + NA_KW - 1, 0, 2 * NA_KW - 2)
    rpb_f = rpb.astype(jnp.float32)
    scale = HEAD_DIM ** -0.5

    def row_fn(r):
        rstart = jnp.clip(r - kh // 2, 0, rows - kh)
        qr = lax.dynamic_index_in_dim(qg, r, axis=1, keepdims=False)
        kr = lax.dynamic_slice_in_dim(kg, rstart, kh, axis=1)
        vr = lax.dynamic_slice_in_dim(vg, rstart, kh, axis=1)
        s = jnp.einsum('bqhd,brkhd->bhqrk', qr, kr).astype(jnp.float32) * scale
        row_idx = rstart + jnp.arange(kh) - r + NA_KH - 1
        bias = rpb_f[:, row_idx[None, :, None], col_idx[:, None, :]]
        s = jnp.where(col_valid[:, None, :], s + bias, -jnp.inf)
        p = jax.nn.softmax(s.reshape(B, B_HEADS, GRID_W, kh * GRID_W), axis=-1)
        p = p.reshape(B, B_HEADS, GRID_W, kh, GRID_W).astype(v.dtype)
        return jnp.einsum('bhqrk,brkhd->bqhd', p, vr)

    out = lax.map(row_fn, jnp.arange(rows))
    return out.transpose(1, 0, 2, 3, 4).reshape(B, S, B_HEADS * HEAD_DIM)

def _retention_dir(q, k, v, log_gamma, strict):
    B, S, H, dk = q.shape
    dv = v.shape[-1]
    nc = S // RET_CHUNK
    dt = q.dtype

    def chunks(t):
        return t.reshape(B, nc, RET_CHUNK, H, t.shape[-1]).transpose(1, 0, 3, 2, 4)

    lg = log_gamma[:, None]
    pos = jnp.arange(RET_CHUNK, dtype=jnp.float32)
    diff = pos[:, None] - pos[None, :]
    allowed = (diff > 0) if strict else (diff >= 0)
    dmask = jnp.where(allowed[None], jnp.exp(lg[:, :, None] * jnp.maximum(diff, 0.0)[None]), 0.0).astype(dt)
    cross = jnp.exp(lg * (pos + 1.0)).astype(dt)
    zeta = jnp.exp(lg * (RET_CHUNK - 1.0 - pos)).astype(dt)
    chunk_decay = jnp.exp(log_gamma * RET_CHUNK).astype(dt)

    def step(R, inp):
        qc, kc, vc = inp
        a = jnp.einsum('bhid,bhjd->bhij', qc, kc) * dmask
        o = jnp.einsum('bhij,bhjv->bhiv', a, vc) + jnp.einsum('bhid,bhdv->bhiv', qc, R) * cross[:, :, None]
        R = R * chunk_decay[:, None, None] + jnp.einsum('bhjd,bhjv->bhdv', kc * zeta[:, :, None], vc)
        return R, o

    R0 = jnp.zeros((B, H, dk, dv), dt)
    _, o = lax.scan(step, R0, (chunks(q), chunks(k), chunks(v)))
    return o.transpose(1, 0, 3, 2, 4).reshape(B, S, H, dv)

def _even_mixer(x, norm_g, w_in, qn_a, kn_a, sink_a, qn_b, kn_b, rpb_b, w_out):
    B, S, _ = x.shape
    h = _rmsnorm(x, norm_g)
    qa, ka, va, qb, kb, vb = _split(h @ w_in, EVEN_SPLITS)
    qa = _rmsnorm(qa.reshape(B, S, A_KV_HEADS, A_GROUP, HEAD_DIM), qn_a)
    ka = _rmsnorm(ka.reshape(B, S, A_KV_HEADS, HEAD_DIM), kn_a)
    va = va.reshape(B, S, A_KV_HEADS, HEAD_DIM)
    oa = _window_gqa(qa, ka, va, sink_a)
    qb = _rmsnorm(qb.reshape(B, S, B_HEADS, HEAD_DIM), qn_b)
    kb = _rmsnorm(kb.reshape(B, S, B_HEADS, HEAD_DIM), kn_b)
    vb = vb.reshape(B, S, B_HEADS, HEAD_DIM)
    ob = _neighbourhood_attn(qb, kb, vb, rpb_b)
    return jnp.concatenate([oa, ob], axis=-1) @ w_out

def _odd_mixer(x, norm_g, w_in, dec_f, dec_b, gn_g, w_out):
    B, S, _ = x.shape
    h = _rmsnorm(x, norm_g)
    q, k, v, g = _split(h @ w_in, ODD_SPLITS)
    q = q.reshape(B, S, RET_HEADS, RET_DK)
    k = k.reshape(B, S, RET_HEADS, RET_DK) * (RET_DK ** -0.5)
    v = v.reshape(B, S, RET_HEADS, RET_DV)
    lgf = jax.nn.log_sigmoid(dec_f.astype(jnp.float32))
    lgb = jax.nn.log_sigmoid(dec_b.astype(jnp.float32))
    y_f = _retention_dir(q, k, v, lgf, False)
    y_b = jnp.flip(_retention_dir(jnp.flip(q, 1), jnp.flip(k, 1), jnp.flip(v, 1), lgb, True), 1)
    yf = (y_f + y_b).astype(jnp.float32)
    mu = jnp.mean(yf, axis=-1, keepdims=True)
    var = jnp.mean(jnp.square(yf - mu), axis=-1, keepdims=True)
    yn = (yf - mu) * lax.rsqrt(var + GN_EPS) * gn_g.astype(jnp.float32).reshape(RET_HEADS, RET_DV)
    yn = yn.astype(x.dtype).reshape(B, S, ODD_MIX)
    return (jax.nn.silu(g) * yn) @ w_out

def _mlp(x, norm_g, w1, w2):
    h = _rmsnorm(x, norm_g)
    return jnp.square(jax.nn.relu(h @ w1)) @ w2

def second_inputs(seed: int = 0) -> dict:
    key = jax.random.key(seed)
    ks = jax.random.split(key, 20)
    f32 = jnp.float32

    def nrm(k, shape, scale):
        return jax.random.normal(k, shape, f32) * scale

    def gain(k, shape):
        return 1.0 + 0.02 * jax.random.normal(k, shape, f32)

    hr = jnp.arange(RET_HEADS, dtype=f32)
    gamma = 1.0 - 2.0 ** (-5.0 - hr)
    base_logit = jnp.log(gamma) - jnp.log1p(-gamma)
    return {
        'x': nrm(ks[0], (BATCH, SEQ, D_MODEL), 1.0),
        'attn_norm_e': gain(ks[1], (N_EVEN, D_MODEL)),
        'w_in_e': nrm(ks[2], (N_EVEN, D_MODEL, EVEN_IN), D_MODEL ** -0.5),
        'q_norm_a': gain(ks[3], (N_EVEN, HEAD_DIM)),
        'k_norm_a': gain(ks[4], (N_EVEN, HEAD_DIM)),
        'sink_a': nrm(ks[5], (N_EVEN, A_Q_HEADS), 0.5),
        'q_norm_b': gain(ks[6], (N_EVEN, HEAD_DIM)),
        'k_norm_b': gain(ks[7], (N_EVEN, HEAD_DIM)),
        'rpb_b': nrm(ks[8], (N_EVEN, B_HEADS, 2 * NA_KH - 1, 2 * NA_KW - 1), 0.02),
        'w_out_e': nrm(ks[9], (N_EVEN, EVEN_MIX, D_MODEL), EVEN_MIX ** -0.5),
        'ret_norm_o': gain(ks[10], (N_ODD, D_MODEL)),
        'w_in_o': nrm(ks[11], (N_ODD, D_MODEL, ODD_IN), D_MODEL ** -0.5),
        'decay_fwd_o': base_logit[None] + nrm(ks[12], (N_ODD, RET_HEADS), 0.05),
        'decay_bwd_o': base_logit[None] + nrm(ks[13], (N_ODD, RET_HEADS), 0.05),
        'ret_gn_o': gain(ks[14], (N_ODD, ODD_MIX)),
        'w_out_o': nrm(ks[15], (N_ODD, ODD_MIX, D_MODEL), ODD_MIX ** -0.5),
        'mlp_norm': gain(ks[16], (DEPTH_2, D_MODEL)),
        'w_mlp_in': nrm(ks[17], (DEPTH_2, D_MODEL, D_FF_2), D_MODEL ** -0.5),
        'w_mlp_out': nrm(ks[18], (DEPTH_2, D_FF_2, D_MODEL), D_FF_2 ** -0.5),
    }

def second_block(x, attn_norm_e, w_in_e, q_norm_a, k_norm_a, sink_a, q_norm_b, k_norm_b, rpb_b, w_out_e,
              ret_norm_o, w_in_o, decay_fwd_o, decay_bwd_o, ret_gn_o, w_out_o,
              mlp_norm, w_mlp_in, w_mlp_out):
    for layer in range(DEPTH_2):
        i = layer // 2
        if layer % 2 == 0:
            x = x + _even_mixer(x, attn_norm_e[i], w_in_e[i], q_norm_a[i], k_norm_a[i], sink_a[i],
                                q_norm_b[i], k_norm_b[i], rpb_b[i], w_out_e[i])
        else:
            x = x + _odd_mixer(x, ret_norm_o[i], w_in_o[i], decay_fwd_o[i], decay_bwd_o[i],
                               ret_gn_o[i], w_out_o[i])
        x = x + _mlp(x, mlp_norm[layer], w_mlp_in[layer], w_mlp_out[layer])
    return x


def setup_inputs(seed=0):
    out = dict(first_inputs(seed))
    for name, value in second_inputs(seed + 1).items():
        if name != "x":
            out[name + "_2"] = value
    return out


def reference(
    x, norm1_g, w_in, attn_q_norm_g, attn_k_norm_g, gla_gate_up, gla_gate_bias, gla_out_norm_g,
    branch_gate_bias, w_attn_branch, w_gla_branch, w_out, norm2_g, w_ff_up, w_ff_down,
    attn_norm_e_2, w_in_e_2, q_norm_a_2, k_norm_a_2, sink_a_2, q_norm_b_2, k_norm_b_2, rpb_b_2,
    w_out_e_2, ret_norm_o_2, w_in_o_2, decay_fwd_o_2, decay_bwd_o_2, ret_gn_o_2, w_out_o_2,
    mlp_norm_2, w_mlp_in_2, w_mlp_out_2,
):
    x = first_block(
        x, norm1_g, w_in, attn_q_norm_g, attn_k_norm_g, gla_gate_up, gla_gate_bias,
        gla_out_norm_g, branch_gate_bias, w_attn_branch, w_gla_branch, w_out, norm2_g, w_ff_up,
        w_ff_down,
    )
    return second_block(
        x, attn_norm_e_2, w_in_e_2, q_norm_a_2, k_norm_a_2, sink_a_2, q_norm_b_2, k_norm_b_2,
        rpb_b_2, w_out_e_2, ret_norm_o_2, w_in_o_2, decay_fwd_o_2, decay_bwd_o_2, ret_gn_o_2,
        w_out_o_2, mlp_norm_2, w_mlp_in_2, w_mlp_out_2,
    )


_drawn_inputs = setup_inputs


def setup_inputs(seed=0):
    import zlib

    import numpy as np

    out = dict(_drawn_inputs(seed))
    spreads = {}
    factors = {'norm1_g': 2.944,
     'attn_q_norm_g': 8.0,
     'attn_k_norm_g': 8.0,
     'gla_gate_bias': 3.038,
     'gla_out_norm_g': 6.776,
     'branch_gate_bias': 3.499,
     'norm2_g': 2.709,
     'attn_norm_e_2': 8.0,
     'q_norm_a_2': 8.0,
     'k_norm_a_2': 8.0,
     'sink_a_2': 4.782,
     'q_norm_b_2': 8.0,
     'k_norm_b_2': 8.0,
     'rpb_b_2': 38.458,
     'ret_norm_o_2': 4.055,
     'ret_gn_o_2': 27.605,
     'mlp_norm_2': 2.72}
    for name, (base, spread) in spreads.items():
        noise = np.random.default_rng([zlib.crc32(name.encode()), seed]).standard_normal(out[name].shape)
        drawn = base * np.exp(spread * noise) if base else spread * noise
        out[name] = __import__('jax').numpy.asarray(drawn.astype(out[name].dtype))
    for name, factor in factors.items():
        out[name] = (out[name] * factor).astype(out[name].dtype)
    return out
```

```python
from contextlib import ExitStack

import concourse.bass as bass
from concourse import mybir

F32 = mybir.dt.float32
F32R = mybir.dt.float32r
ALU = mybir.AluOpType
ACT = mybir.ActivationFunctionType
AX = mybir.AxisListType

P = 128
SEQ = 512
D = 1024
KD = D // P
NT = SEQ // P
FF = 4 * D
FB = FF // D
EPS = 1e-6
GN_EPS = 1e-5
NEG = -1.0e30

E = 64
QKV = 3 * 24 * E
QG, KG, VG = QKV, QKV + 512, QKV + 1024
RG, PA, GATE = QKV + 2048, QKV + 3072, QKV + 3088
GROUPS = 3
QA, KA, VA, QB, KB, VB = 0, 512, 640, 768, 1280, 1792
HEADS = 8

VEC = {}
for name, tiles in (("norm1_g", 8), ("norm2_g", 8), ("attn_norm_e_2", 8), ("ret_norm_o_2", 8), ("mlp_norm_2", 16),
                    ("gla_out_norm_g", 2), ("branch_gate_bias", 16), ("ret_gn_o_2", 16)):
    VEC[name] = sum(n for _, n in VEC.values()), tiles
VROWS = sum(n for _, n in VEC.values())
HEADVEC = ["attn_q_norm_g", "attn_k_norm_g", "q_norm_a_2", "k_norm_a_2", "q_norm_b_2", "k_norm_b_2"]
VALL = VROWS + len(HEADVEC)

WEIGHTS = ["w_in", "w_attn_branch", "w_gla_branch", "w_out", "w_ff_up", "w_ff_down", "w_in_e_2", "w_out_e_2",
           "w_in_o_2", "w_out_o_2", "w_mlp_in_2", "w_mlp_out_2"]


class Count:

    def __init__(self):
        self.n = 0
        self.loop = 0

    def up(self):
        self.n += 1
        return self.n + self.loop


def plan():
    units = []
    steps = {}

    def pipeline(name, todo):
        out = steps.setdefault(name, [])
        prev = None
        for spec, part in todo:
            part = part if isinstance(part, list) else [part] if part else []
            if spec is not None:
                units.append(spec)
                out.append((len(units) - 1, prev, part))
                prev = len(units) - 1
            else:
                out.append((None, prev, part))
                prev = None
        if prev is not None:
            out.append((None, prev, []))

    def ff(i, w1, w2, row):
        steps[f"ff{i}"] = len(units)
        for f in range(FB):
            for j in range(KD):
                units.append(("up", w1, row, f * D + P * j, KD, j))
            for j in range(KD):
                units.append(("down", w2, row * 4 + f * D, P * j, KD, j))

    def beside(specs, parts):
        n = len(specs)
        return [(s, parts[len(parts) * i // n:len(parts) * (i + 1) // n]) for i, s in enumerate(specs)]

    if "1" in MIXERS:
        w = "w_in"
        dil = [[("att", "dil", s, k) for k in range(4)] for s in range(32 + ATT["dil"][1])]

        def three(p):
            return ([("head", w, 0, 512 * g + P * p, KD, ("d", "q", p, g)) for g in range(GROUPS)]
                    + [("head", w, 0, 1536 + 512 * g + P * p, KD, ("d", "k", p, g)) for g in range(GROUPS)]
                    + [("turn", w, 0, 3072 + 512 * g + P * p, KD, ("d", p, g)) for g in range(GROUPS)])

        def gates(branch):
            return [("sigmoid", w, 0, GATE + D * branch + P * j, KD, (branch, j)) for j in range(KD)]

        def gla_head(h):
            return ([("copy", w, 0, QG + P * h, KD, ("gq", h)), ("copy", w, 0, KG + P * h, KD, ("gk", h))]
                    + [("turn", w, 0, VG + 2 * P * h + P * i, KD, ("g", h, i)) for i in range(2)]
                    + [("silu", w, 0, RG + 2 * P * h + P * i, KD, ("g", h, i)) for i in range(2)])

        todo = [(s, [("mask",)] if i == 1 else None) for i, s in enumerate(three(0))]
        for p in range(1, 4):
            q = dil[8 * (p - 1):8 * p]
            todo += zip(three(p), [q[0] + q[1]] + q[2:] + [None, None])
        q = dil[24:]
        todo += zip(gates(0), [q[0] + q[1]] + q[2:8] + [q[8] + q[9]])
        todo += [(("copy", w, 0, PA, KD, ("pa", 0)), [("heads_out", -1, i) for i in range(4)])]
        gla = [[[("gla", h, i), ("gla", h, i + 1)] for i in range(0, 12, 2)] for h in range(4)]
        todo += zip([("branch", "w_attn_branch", 0, P * j, 4, (0, j)) for j in range(KD)],
                    [None, ("lg", 0), None, ("lg", 1), None, ("lg", 2), None, ("lg", 3)])
        todo += [(s, None) for s in gla_head(0)]
        for h in range(1, 4):
            todo += zip(gla_head(h), gla[h - 1])
        todo += zip(gates(1), gla[3] + [None, None])
        todo += [(("branch", "w_gla_branch", 0, P * j, KD, (1, j)), None) for j in range(KD)]
        todo += [(("mix", "w_out", 0, P * j, KD, j), None) for j in range(KD)]
        pipeline("l1", todo)
    if "1" not in MIXERS:
        pipeline("l1", [(("drop", "w_ff_up", 0, 0, KD, 0), None)] * 4)
    ff(0, "w_ff_up", "w_ff_down", 0)

    if "2" in MIXERS:
        w = "w_in_e_2"

        def pair(p):
            return [("head", w, 0, QB + P * p, KD, ("b", "q", p)), ("head", w, 0, KB + P * p, KD, ("b", "k", p)),
                    ("turn", w, 0, VB + P * p, KD, ("b", p))]

        def w_out_e(half):
            return [("down", "w_out_e_2", 512 * half, P * j, 4, j) for j in range(KD)]

        specs = ([("head", w, 0, QA + P * i, KD, ("a", "q", i)) for i in range(4)]
                 + [("head", w, 0, KA, KD, ("a", "k", 0)), ("turn", w, 0, VA, KD, ("a", 0))])
        todo = beside(specs, [("bias", 0, i) for i in range(-1, 8)])
        todo += beside(pair(0) + pair(1), [("att", "win", i) for i in range(32 + ATT["win"][1])])
        todo += [(None, [("heads_out", 0, i)]) for i in range(4)]
        todo += [(None, [("bias", 1, i) for i in range(8)])]
        near = [("att", "near", i) for i in range(32 + ATT["near"][1])]
        todo += [(None, near[0:8])]
        for p in (2, 3):
            n = 8 * (p - 1)
            todo += list(zip(pair(p), (near[n:n + 3], near[n + 3:n + 6], near[n + 6:n + 8])))
        todo += beside(w_out_e(0), near[24:])
        todo += [(None, [("heads_out", 1, i)]) for i in range(4)]
        todo += [(s, None) for s in w_out_e(1)]
        pipeline("l2", todo)
    ff(1, "w_mlp_in_2", "w_mlp_out_2", 0)

    if "3" in MIXERS:
        def head(h):
            w = "w_in_o_2"
            return ([("copy", w, 0, P * h, KD, ("q", h)), ("copy", w, 0, D + P * h, KD, ("k", h))]
                    + [("turn", w, 0, 2 * D + 2 * P * h + P * i, KD, (h, i)) for i in range(2)]
                    + [("silu", w, 0, 4 * D + 2 * P * h + P * i, KD, (h, i)) for i in range(2)])

        def w_out(half):
            return [("down", "w_out_o_2", D * half, P * j, KD, j) for j in range(KD)]

        ret = [[("ret", h, i) for i in range(6)] for h in range(HEADS)]
        todo = [(s, None) for s in head(0)]
        for h in range(1, 5):
            todo += zip(head(h), ret[h - 1])
        todo += zip(w_out(0), ret[4][:4] + [None] * 4)
        todo += zip(head(5), ret[4][4:] + [None] * 4)
        todo += zip(head(6), ret[5])
        todo += zip(head(7), ret[6])
        todo += [(None, r) for r in ret[7]]
        todo += [(s, None) for s in w_out(1)]
        pipeline("l3", todo)
    ff(2, "w_mlp_in_2", "w_mlp_out_2", D)
    return units, steps


MIXERS = "123"
ATT = {"win": (2, 3), "near": (2, 3), "dil": (1, 2)}


def build(nc, a, out):
    units, steps = plan()
    weights = {n: a[n].rearrange("a k n -> (a k) n") for n in WEIGHTS}
    with ExitStack() as ctx:
        def sb(name, shape, dt=F32):
            return ctx.enter_context(nc.sbuf_tensor(name, shape, dt))

        def sem(name):
            return ctx.enter_context(nc.semaphore(name))

        x = sb("x", [P, KD, SEQ])
        raw = sb("raw", [P, 4, KD, P])
        whi = sb("whi", [P, 4, KD, P], F32R)
        wlo = sb("wlo", [P, 4, KD, P], F32R)
        hhi = sb("hhi", [P, KD, SEQ], F32R)
        hlo = sb("hlo", [P, KD, SEQ], F32R)
        uhi = sb("uhi", [P, KD, SEQ], F32R)
        ulo = sb("ulo", [P, KD, SEQ], F32R)
        stage = sb("stage", [P, 2, SEQ])
        tmp = sb("tmp", [P, 2, SEQ])
        ident = sb("ident", [P, P])
        ones = sb("ones", [P, P])
        bones = sb("bones", [P, P])
        vec = sb("vec", [P, P])
        const = sb("const", [P, 4])
        nbias = sb("nbias", [P, 16])
        arena = sb("arena", [P, 17000])
        psum = ctx.enter_context(nc.psum_tensor("psum", [P, 8, 512], F32))
        MB = psum[:, 7, :]
        eps = const[:, 0:1]

        def gain(name, k, tiles=0):
            c = VEC[name][0] + k
            return vec[:, c:c + 1]

        raw_in = [sem(f"raw_in{i}") for i in range(4)]
        hi_done, lo_done = sem("hi_done"), sem("lo_done")
        unit_done, evacuated, posted = sem("unit_done"), sem("evacuated"), sem("posted")
        x_in, vec_in = sem("x_in"), sem("vec_in")
        const_done, x_turned = sem("const_done"), sem("x_turned")
        x_ready, vec_ready = sem("x_ready"), sem("vec_ready")
        dve_step, act_step = sem("dve_step"), sem("act_step")
        norm_sq, norm_sum, norm_rstd = sem("norm_sq"), sem("norm_sum"), sem("norm_rstd")
        norm_h, norm_hi, norm_lo = sem("norm_h"), sem("norm_hi"), sem("norm_lo")
        out_turned, out_copied, out_done = sem("out_turned"), sem("out_copied"), sem("out_done")

        xin = arena[:, 0:NT * D].rearrange("p (t d) -> p t d", t=NT)
        rows = arena[:, 4096:4096 + P]
        hn = arena[:, 0:KD * SEQ].rearrange("p (k t) -> p k t", k=KD)
        xout = arena[:, 4096:4096 + NT * D].rearrange("p (t d) -> p t d", t=NT)

        NORMS = [("l1", "norm1_g", 0), ("ff0", "norm2_g", 0), ("l2", "attn_norm_e_2", 0), ("ff1", "mlp_norm_2", 0),
                 ("l3", "ret_norm_o_2", 0), ("ff2", "mlp_norm_2", KD)]
        NORMS = [n for n in NORMS if n[0] in steps]
        ORDER = {n[0]: i for i, n in enumerate(NORMS)}

        def first(name):
            return steps[name] if name.startswith("ff") else steps[name][0][0]

        shared = [u for u, s in enumerate(units) if s[0] in ("turn", "head")]
        shared_before = {u: shared[i - 1] if i else None for i, u in enumerate(shared)}
        CONSTS = 8
        HALVINGS = (64, 32, 16, 8, 4, 2, 1)
        ARENA = 17000

        UNIT_OF = {s[:4]: u for u, s in enumerate(units)}
        XB = psum[:, 6, :]

        at = [0]

        def place(*shape):
            n = 1
            for d in shape:
                n *= d
            v = arena[:, at[0]:at[0] + n]
            at[0] += n
            assert at[0] <= ARENA, at[0]
            if len(shape) == 2:
                v = v.rearrange("p (a b) -> p a b", a=shape[0])
            return v

        r_q, r_k = [place(SEQ) for _ in range(2)], [place(SEQ) for _ in range(2)]
        r_v = [place(NT, 2 * P) for _ in range(2)]
        r_g = [place(2, SEQ) for _ in range(2)]
        r_dist, r_exp = place(7 * P), place(7 * P)
        r_decay = [place(7 * P) for _ in range(2)]
        r_a = place(NT, SEQ)
        r_y, r_sq = place(2, SEQ), place(2, SEQ)
        r_rstd = place(SEQ)
        r_lg, r_lt = place(16), place(16)
        rate_in, rate_ready, dist_ready = sem("rate_in"), sem("rate_ready"), sem("dist_ready")
        ret_exp, ret_decay, ret_qk, ret_a = sem("ret_exp"), sem("ret_decay"), sem("ret_qk"), sem("ret_a")
        ret_pv, ret_y, ret_mean, ret_yc = sem("ret_pv"), sem("ret_y"), sem("ret_mean"), sem("ret_yc")
        ret_sq, ret_var, ret_rstd, ret_out = sem("ret_sq"), sem("ret_var"), sem("ret_rstd"), sem("ret_out")
        turned, head_sum, head_rstd = sem("turned"), sem("head_sum"), sem("head_rstd")
        at[0] = 0
        d_q, d_k, d_v = [], [], []
        for _ in range(2):
            d_q.append(place(GROUPS, SEQ))
            d_k.append(place(GROUPS, SEQ))
            d_v.append(place(NT, GROUPS * P))
        d_bias = place(256 + 1024)
        d_p = [place(1280) for _ in range(2)]
        d_pt = [place(1280)]
        d_heads = place(NT, 8 * E)
        d_pick = place(2, P)
        at[0] = 0
        mixed = place(KD, SEQ)

        def gla_head_places():
            return place(SEQ), place(SEQ), place(NT, 2 * P), place(2, SEQ)

        gate1_at = at[0]
        g_head = [gla_head_places()]
        g_lg = place(NT, 4 * P)
        g_head.append(gla_head_places())
        g_b = place(SEQ)
        g_e, g_qe = [place(SEQ) for _ in range(2)], [place(SEQ) for _ in range(2)]
        g_a = place(NT, P)
        g_small = place(6, P)
        g_state, g_kt = place(2 * P), place(NT, P)
        g_last = place(NT)
        gate1 = arena[:, gate1_at:gate1_at + KD * SEQ].rearrange("p (k t) -> p k t", k=KD)
        g_pa, g_up = g_kt.rearrange("p a b -> p (a b)"), g_a.rearrange("p a b -> p (a b)")
        tri = sb("tri", [P, P])
        g_mask = sb("g_mask", [P, 6, 32])
        pick_ready, mask_sums, mask_copied, mask_ready = (sem("pick_ready"), sem("mask_sums"), sem("mask_copied"),
                                                          sem("mask_ready"))
        up_in, pa_ones, lg_pe, lg_ln, lg_done = sem("up_in"), sem("pa_ones"), sem("lg_pe"), sem("lg_ln"), sem("lg_done")
        gl_b_pe, gl_b, gl_d, gl_e, gl_f = sem("gl_b_pe"), sem("gl_b"), sem("gl_d"), sem("gl_e"), sem("gl_f")
        gl_level, gl_a, gl_kt_pe, gl_kt = sem("gl_level"), sem("gl_a"), sem("gl_kt_pe"), sem("gl_kt")
        gl_upd, gl_state, gl_pv, gl_o = sem("gl_upd"), sem("gl_state"), sem("gl_pv"), sem("gl_o")
        gl_sq, gl_sum, gl_rstd, gl_out = sem("gl_sq"), sem("gl_sum"), sem("gl_rstd"), sem("gl_out")

        at[0] = 0
        e_q, e_k, e_k2, e_v = place(4, SEQ), place(SEQ), place(SEQ), place(NT, P)
        near_bias = [place(4 * 14 * 64), arena[:, 0:4 * 14 * 64]]
        n_q, n_k = [place(SEQ) for _ in range(2)], [place(SEQ) for _ in range(2)]
        n_v = [place(NT, P) for _ in range(2)]
        win_dist, win_bias = place(3 * P), [place(3 * P) for _ in range(2)]
        heads = place(NT, 8 * E)
        e_p = [place(SEQ) for _ in range(3)]
        e_pt = [place(SEQ) for _ in range(2)]
        rpb_rows, rpb_cols, select = place(31), place(8 * 14), place(192)
        sinks, sinks_neg = place(8), place(8)
        sink_in, rpb_in, near_made = sem("sink_in"), sem("rpb_in"), sem("near_made")
        near_masked, near_sums, win_ready, sel_ready = sem("near_masked"), sem("near_sums"), sem("win_ready"), sem("sel_ready")
        rpb_turned, rpb_ready, dist_pool, dist_abs = sem("rpb_turned"), sem("rpb_ready"), sem("dist_pool"), sem("dist_abs")
        win_made, sink_ready = sem("win_made"), sem("sink_ready")

        cols = sb("cols", [P, 4, 4])
        att_qk, att_sm, att_max, att_exp = sem("att_qk"), sem("att_sm"), sem("att_max"), sem("att_exp")
        att_t, att_copy, att_pv, att_o = sem("att_t"), sem("att_copy"), sem("att_pv"), sem("att_o")
        out_pe, out_hi, out_lo = sem("out_pe"), sem("out_hi"), sem("out_lo")

        items = []
        run_at = {}

        def unit_of(*key):
            return UNIT_OF[key]

        if "l1" in steps:
            run_at["dil"] = len(items)
            for h in range(HEADS):
                r = slice(64 * (h % 2), 64 * (h % 2) + 64)
                buf = (h // 2) % 2
                for n in range(NT):
                    segments, values, c0 = [], [], 0
                    for g in range(GROUPS):
                        lo = max(n - 1, 0) if g == 0 else 0
                        w = (n + 1 - lo) * P
                        end = 256 if g == 0 else 256 + 512 * g
                        segments.append((c0, g, d_q[buf][r, g, P * n:P * n + P], d_k[buf][r, g, P * lo:P * (n + 1)],
                                         d_bias[:, end - w:end]))
                        values += [d_v[buf][:, b, P * g + E * (h % 2):P * g + E * (h % 2) + E] for b in range(lo, n + 1)]
                        c0 += w
                    items.append(dict(run="dil", h=h, width=c0, scale=E ** -0.5, segments=segments, values=values, sink=None,
                                      out=d_heads[:, n, E * h:E * h + E], unit=UNIT_OF["turn", "w_in", 0, 4096 + P * (h // 2)]))
        if "l2" in steps:
            run_at["win"] = len(items)
            for h in range(HEADS):
                r = slice(64 * (h % 2), 64 * (h % 2) + 64)
                keys = e_k if h // 4 == h % 2 else e_k2
                for n in range(NT):
                    lo, hi = max(n - 1, 0), min(n + 2, NT)
                    items.append(dict(
                        run="win", h=h, width=(hi - lo) * P, scale=E ** -0.5,
                        segments=[(0, len(items) % 3, e_q[r, h // 2, P * n:P * n + P], keys[r, P * lo:P * hi],
                                   win_bias[h % 2][:, P * (lo - n + 1):P * (hi - n + 1)])],
                        values=[e_v[:, b, E * (h // 4):E * (h // 4) + E] for b in range(lo, hi)], sink=h,
                        out=heads[:, n, E * h:E * h + E], unit=UNIT_OF["turn", "w_in_e_2", 0, VA]))
            run_at["near"] = len(items)
            for h in range(HEADS):
                r = slice(64 * (h % 2), 64 * (h % 2) + 64)
                p = h // 2
                for n in range(NT):
                    j = (h % 4) * 14 + 6 - 2 * n
                    items.append(dict(
                        run="near", h=h, width=SEQ, scale=E ** -0.5,
                        segments=[(0, len(items) % 3, n_q[p % 2][r, P * n:P * n + P], n_k[p % 2][r, :],
                                   near_bias[h // 4][:, 64 * j:64 * (j + 8)])],
                        values=[n_v[p % 2][:, b, E * (h % 2):E * (h % 2) + E] for b in range(NT)], sink=None,
                        out=heads[:, n, E * h:E * h + E], unit=UNIT_OF["turn", "w_in_e_2", 0, VB + P * p]))
        run_n = {r: sum(it["run"] == r for it in items) for r in run_at}
        rounds = [0]
        for it in items:
            rounds.append(rounds[-1] + -(-len(it["values"]) // 4))
            it["p"] = e_p if it["run"] != "dil" else d_p
            it["pt"] = e_pt if it["run"] != "dil" else d_pt
        GL = 8
        OUT0 = 4 if "l1" in steps else 0

        def out_index(half, i):
            return i if half < 0 else OUT0 + 4 * half + i

        TURNS = {u: i for i, u in enumerate(u for u, s in enumerate(units) if s[0] == "turn")}
        HEADU = {u: i for i, u in enumerate(u for u, s in enumerate(units) if s[0] == "head")}

        block = ctx.enter_context(nc.Block())

        @block.sync
        def _(sp):
            sp.dma_start(xin, a["x"][0].rearrange("(t p) d -> p t d", p=P)).then_inc(x_in, 16)
            for name, (r0, n) in VEC.items():
                sp.dma_start(rows[r0:r0 + n, :], a[name].rearrange("a (n p) -> (a n) p", p=P)).then_inc(vec_in, 16)
            for i, name in enumerate(HEADVEC):
                for half in range(2):
                    sp.dma_start(rows[VROWS + i:VROWS + i + 1, 64 * half:64 * half + 64], a[name]).then_inc(vec_in, 16)

            def load(u, row=0, col=0, more=0):
                _, name, row0, col0, kt, _ = units[u]
                if u >= 4:
                    sp.wait_ge(hi_done, u - 3 + more)
                    sp.wait_ge(lo_done, u - 3 + more)
                src = weights[name][bass.ds(row0 + row, kt * P), bass.ds(col0 + col, P)]
                sp.dma_start(raw[:, u % 4, 0:kt, :], src.rearrange("(k p) c -> p k c", p=P)).then_inc(raw_in[u % 4], 16)

            def static(name):
                for u, _, _ in steps[name]:
                    if u is not None:
                        load(u)

            def ff(i):
                with sp.Fori(0, FB) as f:
                    for j in range(16):
                        load(steps[f"ff{i}"] + j, 0 if j < 8 else f * D, f * D if j < 8 else 0, f * 16)

            for name, _, _ in NORMS:
                if name.startswith("ff"):
                    ff(int(name[2]))
                else:
                    static(name)
            for t in range(NT):
                sp.wait_ge(out_copied, 2 * t + 2)
                sp.dma_start(out[0, P * t:P * t + P, :], xout[:, t, :]).then_inc(out_done, 16)
            sp.wait_ge(out_done, 16 * NT)

        @block.gpsimd
        def _(pool):
            count = Count()

            def done(ins):
                ins.then_inc(const_done, 1)
                pool.wait_ge(const_done, count.up())

            done(pool.memset(ones[:, :], 1.0))
            done(pool.memset(const[:, 0:1], EPS))
            done(pool.memset(const[:, 1:2], GN_EPS))
            done(pool.memset(bones[:, :], 0.0))
            for i in range(2):
                done(pool.memset(bones[64 * i:64 * i + 64, 64 * i:64 * i + 64], 1.0))
            done(pool.memset(ident[:, :], 0.0))
            done(pool.affine_select(out=ident[:, :], in_=ident[:, :], compare_op=ALU.not_equal, fill=1.0, base=0,
                                    pattern=[[-1, P]], channel_multiplier=1))
            if "l1" in steps:
                done(pool.memset(tri[:, :], 1.0))
                done(pool.affine_select(out=tri[:, :], in_=tri[:, :], compare_op=ALU.is_ge, fill=0.0, base=0,
                                        pattern=[[1, P]], channel_multiplier=-1))
                done(pool.memset(g_mask[:, :, :], 0.0))
                for i, m in enumerate(HALVINGS[2:]):
                    v = g_mask[:, i, :].rearrange("p (b h w) -> p b h w", h=2, w=m)[:, :, 1, :]
                    done(pool.memset(v, 1.0))
                    for j in range(4):
                        r = v[32 * j:32 * j + 32]
                        done(pool.affine_select(out=r, in_=r, compare_op=ALU.is_ge, fill=0.0, base=0,
                                                pattern=[[-2 * m, 16 // m], [0, m]], channel_multiplier=1))
                        done(pool.affine_select(out=r, in_=r, compare_op=ALU.is_ge, fill=0.0, base=m - 1,
                                                pattern=[[2 * m, 16 // m], [0, m]], channel_multiplier=-1))
                for j in range(4):
                    r = g_mask[32 * j:32 * j + 32, 5, :]
                    done(pool.affine_select(out=r, in_=r, compare_op=ALU.not_equal, fill=1.0, base=0,
                                            pattern=[[-1, 32]], channel_multiplier=1))
                pool.wait_ge(norm_lo, KD)
                done(pool.memset(d_pick, 0.0))
                for i, m in enumerate((4, 16)):
                    v = d_pick[0:m, i, :].rearrange("p (a b) -> p a b", b=m)
                    done(pool.affine_select(out=v, in_=v, compare_op=ALU.not_equal, fill=1.0, base=0,
                                            pattern=[[0, P // m], [-1, m]], channel_multiplier=1))
                pool.sem_inc(pick_ready, 1)
                pool.wait_ge(mask_copied, 1)
                v = d_bias[:, 0:P]
                done(pool.affine_select(out=v, in_=v, compare_op=ALU.is_ge, fill=NEG, base=0, pattern=[[1, P]],
                                        channel_multiplier=-1))
                for c in (P, 256 + 3 * P, 256 + 7 * P):
                    v = d_bias[:, c:c + P]
                    done(pool.affine_select(out=v, in_=v, compare_op=ALU.is_ge, fill=NEG, base=0, pattern=[[-1, P]],
                                            channel_multiplier=1))
                pool.sem_inc(mask_ready, 1)
                pool.wait_ge(att_o, run_at["dil"] + 32)
                pool.wait_ge(out_lo, 4)
                done(pool.memset(g_pa[0:32, :], 1.0))
                pool.sem_inc(pa_ones, 1)
            if "l2" in steps:
                pool.wait_ge(norm_lo, KD * (ORDER["l2"] + 1))
                done(pool.memset(select, 0.0))
                for i in range(2):
                    z = select[32 * i:32 * i + 32, :]
                    done(pool.affine_select(out=z, in_=z, compare_op=ALU.not_equal, fill=1.0, base=-78,
                                            pattern=[[1, 192]], channel_multiplier=1))
                done(pool.iota(win_dist, pattern=[[1, 3 * P]], base=-P, channel_multiplier=-1,
                               allow_small_or_imprecise_dtypes=True))
                pool.sem_inc(dist_pool, 1)
                pool.wait_ge(dist_abs, 1)
                for sign in (1, -1):
                    done(pool.affine_select(out=win_dist, in_=win_dist, compare_op=ALU.is_ge, fill=-NEG, base=P - sign * P,
                                            pattern=[[sign, 3 * P]], channel_multiplier=-sign))
                pool.sem_inc(dist_pool, 1)
                for half in range(2):
                    pool.wait_ge(near_made, 8 * (half + 1))
                    b = near_bias[half].rearrange("p (q c) -> p q c", c=64)
                    for i in range(2):
                        r = slice(64 * i, 64 * i + 64)
                        v = b[r, :, 0:48]
                        done(pool.affine_select(out=v, in_=v, compare_op=ALU.is_ge, fill=NEG, base=8,
                                                pattern=[[0, 56], [1, 48]], channel_multiplier=-1))
                        v = b[r, :, 16:64]
                        done(pool.affine_select(out=v, in_=v, compare_op=ALU.is_ge, fill=NEG, base=7 - 16,
                                                pattern=[[0, 56], [-1, 48]], channel_multiplier=1))
                    pool.sem_inc(near_masked, 1)
            if "l3" in steps:
                pool.wait_ge(norm_lo, KD * (ORDER["l3"] + 1))
                pool.iota(r_dist, pattern=[[1, 7 * P]], base=-3 * P, channel_multiplier=-1,
                          allow_small_or_imprecise_dtypes=True).then_inc(dist_ready, 1)

        @block.scalar
        def _(act):
            chain = Count()

            def split_hi(u, more=0):
                kt = units[u][4] if u < len(units) else KD
                act.wait_ge(raw_in[u % 4], 16 * (u // 4 + 1) + more * 4)
                if u >= 4:
                    act.wait_ge(unit_done, u - 3 + more)
                nc.scalar.copy(whi[:, u % 4, 0:kt, :], raw[:, u % 4, 0:kt, :]).then_inc(hi_done, 1)

            def evacuate(u, more=0):
                act.wait_ge(unit_done, u + 1 + more)
                if u >= 2:
                    act.wait_ge(posted, u - 1 + more)
                kind, which = units[u][0], units[u][5]
                g, s, t = psum[:, u % 2, :], stage[:, u % 2, :], tmp[:, u % 2, :]
                if kind == "silu":
                    nc.scalar.copy(s, g)
                    nc.scalar.activation(t, g, ACT.Exp, scale=-1.0).then_inc(evacuated, 1)
                elif kind == "sigmoid":
                    branch, j = which
                    b = nbias[:, KD * branch + j:KD * branch + j + 1]
                    nc.scalar.activation(t, g, ACT.Exp, scale=-1.0, bias=b).then_inc(evacuated, 1)
                elif kind == "head":
                    nc.scalar.copy(s, g)
                    nc.scalar.activation(t, g, ACT.Square).then_inc(evacuated, 1)
                    act.wait_ge(head_sum, HEADU[u] + 1)
                    nc.scalar.activation(t, XB, ACT.Ln, bias=eps, scale=1.0 / 64).then_inc(act_step, 1)
                    act.wait_ge(act_step, chain.up())
                    nc.scalar.activation(t, t, ACT.Exp, scale=-0.5).then_inc(head_rstd, 1)
                elif kind == "up":
                    nc.scalar.activation(s, g, ACT.Relu).then_inc(evacuated, 1)
                elif kind == "copy" and which[0] in ("k", "gq"):
                    nc.scalar.activation(s, g, ACT.Copy, scale=float(P) ** -0.5).then_inc(evacuated, 1)
                else:
                    nc.scalar.copy(s, g).then_inc(evacuated, 1)

            def decay(h):
                act.wait_ge(ret_exp, h + 1)
                nc.scalar.activation(r_decay[h % 2], r_exp, ACT.Exp).then_inc(ret_decay, 1)

            def ret(h, part):
                if part == 2:
                    act.wait_ge(ret_pv, h + 1)
                    for i in range(2):
                        nc.scalar.copy(r_y[:, i, :], psum[:, 4 + i, :]).then_inc(ret_y, 1)
                if part == 3:
                    act.wait_ge(ret_yc, 2 * h + 2)
                    nc.scalar.activation(r_sq, r_y, ACT.Square).then_inc(ret_sq, 1)
                if part == 4:
                    act.wait_ge(ret_var, h + 1)
                    nc.scalar.activation(r_rstd, MB, ACT.Ln, bias=const[:, 1:2], scale=1.0 / (2 * P)).then_inc(act_step, 1)
                    act.wait_ge(act_step, chain.up())
                    nc.scalar.activation(r_rstd, r_rstd, ACT.Exp, scale=-0.5).then_inc(ret_rstd, 1)
                if part == 5 and h + 1 < HEADS:
                    decay(h + 1)

            def rates():
                act.wait_ge(norm_lo, KD * (ORDER["l3"] + 1))
                for i, rate in enumerate(("decay_fwd_o_2", "decay_bwd_o_2")):
                    act.dma_start(r_lg[:, 8 * i:8 * i + 8], a[rate].partition_broadcast(P)).then_inc(rate_in, 16)
                act.wait_ge(rate_in, 32)
                nc.scalar.activation(r_lt, r_lg, ACT.Abs).then_inc(act_step, 1)
                act.wait_ge(act_step, chain.up())
                nc.scalar.activation(r_lt, r_lt, ACT.Exp, scale=-1.0).then_inc(act_step, 1)
                act.wait_ge(act_step, chain.up())
                nc.scalar.activation(r_lt, r_lt, ACT.Ln, bias=1.0).then_inc(rate_ready, 1)
                decay(0)

            def att(run, s, k=0):
                if k:
                    return
                at, count = run_at[run], run_n[run]
                i = s - ATT[run][0]
                if 0 <= i < count:
                    g = at + i
                    it = items[g]
                    pt = it["pt"][g % len(it["pt"])]
                    n = len(it["values"])
                    for r in range(-(-n // 4)):
                        act.wait_ge(att_t, rounds[g] + r + 1)
                        if r == 0 and g >= len(it["pt"]):
                            act.wait_ge(att_pv, g - len(it["pt"]) + 1)
                        w = P * min(4, n - 4 * r)
                        nc.scalar.copy(pt[:, 512 * r:512 * r + w], psum[:, 5, 0:w]).then_inc(att_copy, 1)
                if s < count:
                    g = at + s
                    it = items[g]
                    p = it["p"][g % len(it["p"])][:, 0:it["width"]]
                    c = cols[:, g % 4, :]
                    act.wait_ge(att_max, g + 1)
                    if g >= 4:
                        act.wait_ge(att_o, g - 3)
                    if it["sink"] is not None:
                        h = it["sink"]
                        nc.scalar.activation(c[:, 2:3], sinks[:, h:h + 1], ACT.Exp, bias=c[:, 0:1])
                    nc.scalar.activation(p, p, ACT.Exp, bias=c[:, 0:1], accum_out=c[:, 1:2]).then_inc(att_exp, 1)

            def gate_up_load():
                act.dma_start(g_up[0:16, :], a["gla_gate_up"][0]).then_inc(up_in, 16)
                act.dma_start(g_up[16:17, :], a["gla_gate_bias"]).then_inc(up_in, 16)

            def heads_out(half, i):
                n = max(4 * half, 0) + i
                m = out_index(half, i)
                act.wait_ge(out_pe, m + 1)
                nc.scalar.copy(uhi[:, n, :], psum[:, 2 + n % 2, :]).then_inc(out_hi, 1)
                if half < 0 and i == 3:
                    act.wait_ge(out_lo, 3)
                    act.wait_ge(out_pe, 4)
                    gate_up_load()

            def lg(t):
                l = g_e[t % 2]
                act.wait_ge(lg_pe, t + 1)
                if t >= 2:
                    act.wait_ge(lg_done, t - 1)
                nc.scalar.activation(l, psum[:, 2 + t, :], ACT.Abs).then_inc(act_step, 1)
                act.wait_ge(act_step, chain.up())
                nc.scalar.activation(l, l, ACT.Exp, scale=-1.0).then_inc(act_step, 1)
                act.wait_ge(act_step, chain.up())
                nc.scalar.activation(l, l, ACT.Ln, bias=1.0).then_inc(lg_ln, 1)

            def gla(h, part):
                if part == 0:
                    act.wait_ge(gl_b_pe, h + 1)
                    nc.scalar.copy(g_b, psum[:, 2, :]).then_inc(gl_b, 1)
                if part < 7 or part == 8:
                    n = min(part, 7)
                    act.wait_ge(gl_d, 8 * h + n + 1)
                    e = g_e[part % 2]
                    nc.scalar.activation(e, e, ACT.Abs).then_inc(act_step, 1)
                    act.wait_ge(act_step, chain.up())
                    nc.scalar.activation(e, e, ACT.Exp, scale=-1.0 / 16).then_inc(gl_e, 1)
                if part == 7:
                    act.wait_ge(gl_level, GL * h + 6)
                    nc.scalar.activation(g_e[1], g_b, ACT.Exp, scale=1.0 / 16)
                    nc.scalar.activation(g_last, g_b.rearrange("p (c t) -> p c t", c=NT)[:, :, P - 1], ACT.Exp,
                                         scale=1.0 / 16).then_inc(gl_e, 1)
                if part == 9:
                    act.wait_ge(gl_kt_pe, h + 1)
                    nc.scalar.copy(g_kt, psum[:, 3, :]).then_inc(gl_kt, 1)
                if part == 10:
                    act.wait_ge(gl_pv, h + 1)
                    for i in range(2):
                        nc.scalar.copy(g_head[h % 2][i], psum[:, 4 + i, :]).then_inc(gl_o, 1)
                if part == 11:
                    for i in range(2):
                        act.wait_ge(gl_o, 2 * h + i + 1)
                        nc.scalar.activation(g_qe[i], g_head[h % 2][i], ACT.Square).then_inc(gl_sq, 1)
                    act.wait_ge(gl_sum, h + 1)
                    nc.scalar.activation(g_b, MB, ACT.Ln, bias=eps, scale=1.0 / (2 * P)).then_inc(act_step, 1)
                    act.wait_ge(act_step, chain.up())
                    nc.scalar.activation(g_b, g_b, ACT.Exp, scale=-0.5).then_inc(gl_rstd, 1)

            def bias(half, i):
                if i < 0:
                    act.wait_ge(dist_pool, 1)
                    nc.scalar.activation(win_dist, win_dist, ACT.Abs).then_inc(dist_abs, 1)
                    return
                act.wait_ge(near_sums, 8 * half + i + 1)
                o = near_bias[half].rearrange("p (q c) -> p q c", c=64)[:, :, 8 * i:8 * i + 8]
                nc.scalar.copy(o, psum[:, 2 + i % 2, 0:448].rearrange("p (c q) -> p q c", c=8)).then_inc(near_made, 1)

            def nothing(*_):
                pass

            PARTS = {"ret": ret, "att": att, "heads_out": heads_out, "bias": bias, "lg": lg, "gla": gla, "mask": nothing}

            def static(name):
                if name == "l3":
                    rates()
                if name == "l1":
                    act.wait_ge(vec_ready, 2)
                if name == "l2":
                    act.wait_ge(norm_lo, KD * (ORDER["l2"] + 1))
                    act.dma_start(sinks, a["sink_a_2"].partition_broadcast(P)).then_inc(sink_in, 16)
                    act.dma_start(rpb_rows[0:120, :], a["rpb_b_2"].rearrange("a h j c -> (a h j) c")).then_inc(rpb_in, 16)
                for u, prev, parts in steps[name]:
                    if u is not None:
                        split_hi(u + 2)
                    if prev is not None:
                        evacuate(prev)
                    for part in parts:
                        PARTS[part[0]](*part[1:])

            def norm(n):
                before = first(NORMS[n][0])
                for k in range(KD):
                    if k == 0:
                        if before:
                            act.wait_ge(posted, before)
                        act.wait_ge(x_ready, KD)
                    else:
                        act.wait_ge(norm_sum, KD * n + k - 1) if k >= 2 else None
                    nc.scalar.activation(tmp[:, k % 2, :], x[:, k, :], ACT.Square).then_inc(norm_sq, 1)
                act.wait_ge(norm_sum, KD * n + KD)
                nc.scalar.activation(tmp[:, 0, :], MB, ACT.Ln, bias=eps, scale=1.0 / D).then_inc(act_step, 1)
                act.wait_ge(act_step, chain.up())
                nc.scalar.activation(tmp[:, 1, :], tmp[:, 0, :], ACT.Exp, scale=-0.5).then_inc(norm_rstd, 1)
                for k in range(KD):
                    act.wait_ge(norm_h, KD * n + k + 1)
                    nc.scalar.copy(hhi[:, k, :], hn[:, k, :]).then_inc(norm_hi, 1)

            def ff_block(b, more, last=False):
                for j in range(16):
                    if not (last and j >= 14):
                        split_hi_ff(b, j + 2, more)
                    if j:
                        evacuate(b + j - 1, more)
                evacuate(b + 15, more)

            def split_hi_ff(b, j, more):
                u = b + j
                act.wait_ge(raw_in[u % 4], 16 * (u // 4 + 1) + more * 4)
                act.wait_ge(unit_done, u - 3 + more)
                nc.scalar.copy(whi[:, u % 4, :, :], raw[:, u % 4, :, :]).then_inc(hi_done, 1)

            def ff(i):
                b = steps[f"ff{i}"]
                with act.Fori(0, FB - (i == 2)) as f:
                    ff_block(b, f * 16)
                if i == 2:
                    ff_block(b, 16 * (FB - 1), last=True)

            act.preload_act_table_set("natural_log_exp_and_others")
            act.wait_ge(const_done, CONSTS)
            split_hi(0)
            split_hi(1)
            for k in range(KD):
                act.wait_ge(x_turned, k + 1)
                nc.scalar.copy(x[:, k, :], psum[:, k % 2, :]).then_inc(x_ready, 1)
            for n, (name, _, _) in enumerate(NORMS):
                norm(n)
                if name.startswith("ff"):
                    ff(int(name[2]))
                else:
                    static(name)
            for n in range(2 * NT):
                act.wait_ge(out_turned, n + 1)
                nc.scalar.copy(xout[:, n // 2, 512 * (n % 2):512 * (n % 2) + 512], psum[:, n % 2, :]).then_inc(out_copied, 1)

        @block.vector
        def _(dve):
            chain = Count()

            def split_lo(u, more=0, kt=KD):
                dve.wait_ge(hi_done, u + 1 + more)
                dve.tensor_tensor(wlo[:, u % 4, 0:kt, :], raw[:, u % 4, 0:kt, :], whi[:, u % 4, 0:kt, :].bitcast(F32),
                                  ALU.subtract).then_inc(lo_done, 1)

            def post(u, more=0):
                kind, _, _, _, _, j = units[u]
                s = stage[:, u % 2, :]
                dve.wait_ge(evacuated, u + 1 + more)
                if kind == "drop":
                    dve.tensor_copy(tmp[:, 0, u:u + 1], s[:, 0:1]).then_inc(posted, 1)
                if kind == "copy":
                    which, h = j
                    if which == "pa":
                        dve.wait_ge(pa_ones, 1)
                        dve.tensor_copy(g_pa[0:16, :], s[0:16, :]).then_inc(posted, 1)
                    elif which in ("gq", "gk"):
                        dve.tensor_copy(g_head[h % 2][which == "gk"], s).then_inc(posted, 1)
                    else:
                        dve.tensor_copy((r_q if which == "q" else r_k)[h % 2], s).then_inc(posted, 1)
                if kind == "sigmoid":
                    branch, i = j
                    t = tmp[:, u % 2, :]
                    if branch == 0 and i == 0:
                        dve.wait_ge(att_o, run_at["dil"] + 24)
                    dve.tensor_scalar(t, t, 1.0, None, ALU.add).then_inc(dve_step, 1)
                    dve.wait_ge(dve_step, chain.up())
                    dve.reciprocal((mixed if branch == 0 else gate1)[:, i, :], t).then_inc(posted, 1)
                if kind == "branch":
                    branch, i = j
                    if branch == 0:
                        dve.tensor_tensor(mixed[:, i, :], mixed[:, i, :], s, ALU.mult).then_inc(posted, 1)
                    else:
                        t = tmp[:, u % 2, :]
                        dve.tensor_tensor(t, gate1[:, i, :], s, ALU.mult).then_inc(dve_step, 1)
                        dve.wait_ge(dve_step, chain.up())
                        dve.tensor_tensor(t, mixed[:, i, :], t, ALU.add).then_inc(dve_step, 1)
                        dve.wait_ge(dve_step, chain.up())
                        dve.tensor_copy(hhi[:, i, :], t).then_inc(dve_step, 1)
                        dve.wait_ge(dve_step, chain.up())
                        dve.tensor_tensor(hlo[:, i, :], t, hhi[:, i, :].bitcast(F32), ALU.subtract).then_inc(posted, 1)
                if kind == "turn":
                    if j[0] == "a":
                        o = e_v
                    elif j[0] == "b":
                        o = n_v[j[1] % 2]
                        if j[1] >= 2:
                            dve.wait_ge(att_o, run_at["near"] + 8 * (j[1] - 1))
                    elif j[0] == "d":
                        o = d_v[j[1] % 2][:, :, P * j[2]:P * j[2] + P]
                    elif j[0] == "g":
                        o = g_head[j[1] % 2][2][:, :, P * j[2]:P * j[2] + P]
                    else:
                        o = r_v[j[0] % 2][:, :, P * j[1]:P * j[1] + P]
                    dve.wait_ge(turned, TURNS[u] + 1)
                    dve.tensor_copy(o, XB.rearrange("p (t c) -> p t c", t=NT)).then_inc(posted, 1)
                if kind == "head":
                    layer, which, i = j[:3]
                    t = tmp[:, u % 2, :]
                    g = VROWS + {"d": 0, "a": 2, "b": 4}[layer] + (which == "k")
                    if layer == "d":
                        o = (d_q if which == "q" else d_k)[i % 2][:, j[3], :]
                        if i >= 2:
                            dve.wait_ge(att_o, run_at["dil"] + 8 * (i - 1))
                    if layer == "a":
                        o = e_q[:, i, :] if which == "q" else e_k
                    if layer == "b":
                        o = (n_q if which == "q" else n_k)[i % 2]
                        if i >= 2:
                            dve.wait_ge(att_o, run_at["near"] + 8 * (i - 1))
                    dve.wait_ge(head_rstd, HEADU[u] + 1)
                    ins = dve.scalar_tensor_tensor(out=o, in0=s, scalar=vec[:, g:g + 1], in1=t, op0=ALU.mult, op1=ALU.mult)
                    if layer == "a" and which == "k":
                        ins.then_inc(dve_step, 1)
                        dve.wait_ge(dve_step, chain.up())
                        dve.tensor_copy(e_k2[0:64, :], e_k[64:128, :]).then_inc(dve_step, 1)
                        dve.wait_ge(dve_step, chain.up())
                        ins = dve.tensor_copy(e_k2[64:128, :], e_k[0:64, :])
                    ins.then_inc(posted, 1)
                if kind == "silu":
                    h, i = j[-2:]
                    dest = g_head[h % 2][3] if j[0] == "g" else r_g[h % 2]
                    t = tmp[:, u % 2, :]
                    dve.tensor_scalar(t, t, 1.0, None, ALU.add).then_inc(dve_step, 1)
                    dve.wait_ge(dve_step, chain.up())
                    dve.reciprocal(t, t).then_inc(dve_step, 1)
                    dve.wait_ge(dve_step, chain.up())
                    dve.tensor_tensor(dest[:, i, :], s, t, ALU.mult).then_inc(posted, 1)
                if kind in ("down", "mix"):
                    dve.tensor_tensor(x[:, j, :], x[:, j, :], s, ALU.add).then_inc(posted, 1)
                if kind == "up":
                    t = tmp[:, u % 2, :]
                    dve.tensor_tensor(t, s, s, ALU.mult).then_inc(dve_step, 1)
                    dve.wait_ge(dve_step, chain.up())
                    dve.tensor_copy(uhi[:, j, :], t).then_inc(dve_step, 1)
                    dve.wait_ge(dve_step, chain.up())
                    dve.tensor_tensor(ulo[:, j, :], t, uhi[:, j, :].bitcast(F32), ALU.subtract).then_inc(posted, 1)

            def decay(h):
                dve.wait_ge(ret_decay, h) if h else dve.wait_ge(dist_ready, 1)
                dve.tensor_scalar(r_exp, r_dist, r_lt[:, 8 + h:9 + h], None, ALU.mult).then_inc(dve_step, 1)
                dve.wait_ge(dve_step, chain.up())
                dve.scalar_tensor_tensor(out=r_exp, in0=r_dist, scalar=r_lg[:, h:h + 1], in1=r_exp,
                                         op0=ALU.mult, op1=ALU.min).then_inc(ret_exp, 1)

            def rates():
                dve.wait_ge(rate_ready, 1)
                dve.scalar_tensor_tensor(out=r_lg, in0=r_lg, scalar=0.0, in1=r_lt, op0=ALU.min,
                                         op1=ALU.subtract).then_inc(dve_step, 1)
                dve.wait_ge(dve_step, chain.up())
                dve.tensor_scalar(r_lt, r_lg, -1.0, None, ALU.mult).then_inc(dve_step, 1)
                dve.wait_ge(dve_step, chain.up())
                decay(0)

            def ret(h, part):
                if part < 2:
                    for j in (2 * part, 2 * part + 1):
                        dve.wait_ge(ret_qk, NT * h + j + 1)
                        if j == 0:
                            dve.wait_ge(ret_decay, h + 1)
                        dve.tensor_tensor(r_a[:, j, :], psum[:, 2 + j % 2, :],
                                          r_decay[h % 2][:, (3 - j) * P:(3 - j) * P + SEQ], ALU.mult).then_inc(ret_a, 1)
                if part == 3:
                    dve.wait_ge(ret_mean, h + 1)
                    for i in range(2):
                        dve.scalar_tensor_tensor(out=r_y[:, i, :], in0=MB, scalar=-1.0 / (2 * P), in1=r_y[:, i, :],
                                                 op0=ALU.mult, op1=ALU.add).then_inc(ret_yc, 1)
                if part == 4:
                    dve.wait_ge(ret_rstd, h + 1)
                    if h == 4:
                        dve.wait_ge(unit_done, UNIT_OF["down", "w_out_o_2", 0, D - P] + 1)
                    for i in range(2):
                        y = r_y[:, i, :]
                        j = 2 * (h % 4) + i
                        dve.scalar_tensor_tensor(out=y, in0=y, scalar=gain("ret_gn_o_2", 2 * h + i), in1=r_rstd,
                                                 op0=ALU.mult, op1=ALU.mult).then_inc(dve_step, 1)
                        dve.wait_ge(dve_step, chain.up())
                        dve.tensor_tensor(y, y, r_g[h % 2][:, i, :], ALU.mult).then_inc(dve_step, 1)
                        dve.wait_ge(dve_step, chain.up())
                        dve.tensor_copy(uhi[:, j, :], y).then_inc(dve_step, 1)
                        dve.wait_ge(dve_step, chain.up())
                        dve.tensor_tensor(ulo[:, j, :], y, uhi[:, j, :].bitcast(F32), ALU.subtract).then_inc(ret_out, 1)
                if part == 5 and h + 1 < HEADS:
                    decay(h + 1)

            def att(run, s, k=0):
                if k:
                    return
                at, count = run_at[run], run_n[run]
                if s < count:
                    g = at + s
                    it = items[g]
                    p = it["p"][g % len(it["p"])]
                    c = cols[:, g % 4, :]
                    if run == "win" and s % NT == 0:
                        h = it["h"]
                        if h == 0:
                            dve.wait_ge(dist_pool, 2)
                        dve.tensor_scalar(win_bias[h % 2], win_dist, -2.0 ** -(h + 1), None, ALU.mult).then_inc(dve_step, 1)
                        dve.wait_ge(dve_step, chain.up())
                    if run == "dil" and s == 0:
                        dve.wait_ge(mask_ready, 1)
                    if run == "near" and s % 16 == 0:
                        dve.wait_ge(near_masked, s // 16 + 1)
                    dve.wait_ge(att_qk, g + 1)
                    if g >= len(it["p"]):
                        dve.wait_ge(att_t, rounds[g - len(it["p"]) + 1])
                    for c0, b, q, k, bias in it["segments"]:
                        w = k.shape[1]
                        ins = dve.scalar_tensor_tensor(out=p[:, c0:c0 + w], in0=psum[:, 2 + b, 0:w], scalar=it["scale"],
                                                       in1=bias, op0=ALU.mult, op1=ALU.add)
                    ins.then_inc(att_sm, 1)
                    dve.wait_ge(att_sm, g + 1)
                    if g >= 4:
                        dve.wait_ge(att_o, g - 3)
                    if it["sink"] is None:
                        dve.tensor_reduce(c[:, 0:1], p[:, 0:it["width"]], AX.X, ALU.max, negate=True).then_inc(att_max, 1)
                    else:
                        dve.tensor_reduce(c[:, 0:1], p[:, 0:it["width"]], AX.X, ALU.max, negate=True).then_inc(dve_step, 1)
                        dve.wait_ge(dve_step, chain.up())
                        h = it["sink"]
                        dve.tensor_tensor(c[:, 0:1], c[:, 0:1], sinks_neg[:, h:h + 1], ALU.min).then_inc(att_max, 1)
                i = s - ATT[run][1]
                if 0 <= i < count:
                    g = at + i
                    it = items[g]
                    c = cols[:, g % 4, :]
                    dve.wait_ge(att_exp, g + 1)
                    den = c[:, 1:2]
                    if it["sink"] is not None:
                        dve.tensor_tensor(c[:, 2:3], den, c[:, 2:3], ALU.add).then_inc(dve_step, 1)
                        dve.wait_ge(dve_step, chain.up())
                        den = c[:, 2:3]
                    dve.reciprocal(c[:, 3:4], den).then_inc(dve_step, 1)
                    dve.wait_ge(dve_step, chain.up())
                    dve.wait_ge(att_pv, g + 1)
                    dve.tensor_scalar(it["out"], MB[:, 0:E], c[:, 3:4], None, ALU.mult).then_inc(att_o, 1)

            def heads_out(half, i):
                n = max(4 * half, 0) + i
                dve.wait_ge(out_hi, out_index(half, i) + 1)
                dve.tensor_tensor(ulo[:, n, :], psum[:, 2 + n % 2, :], uhi[:, n, :].bitcast(F32), ALU.subtract).then_inc(out_lo, 1)

            def mask():
                dve.wait_ge(mask_sums, 1)
                dve.memset(d_bias[:, 0:256], 0.0)
                for i in range(2):
                    for c in range(NT):
                        o = 256 + 512 * i + P * c
                        ins = dve.tensor_scalar(d_bias[:, o:o + P], psum[:, 2, P * i:P * i + P], -NEG, NEG, ALU.mult, ALU.add)
                ins.then_inc(mask_copied, 1)

            def lg(t):
                dve.wait_ge(lg_ln, t + 1)
                dve.scalar_tensor_tensor(out=g_lg[:, t, :], in0=psum[:, 2 + t, :], scalar=0.0, in1=g_e[t % 2],
                                         op0=ALU.min, op1=ALU.subtract).then_inc(lg_done, 1)

            def gla(h, part):
                q, k, v, r = g_head[h % 2]
                k_n = 9 * h
                b3 = g_b.rearrange("p (c t) -> p c t", c=NT)

                def difference(n):
                    m = HALVINGS[n] if n < 7 else P // 2
                    at_ = m - 1 if n < 7 else P - 1
                    blocks = g_b.rearrange("p (b t) -> p b t", t=2 * m)
                    e = g_e[n % 2].rearrange("p (b t) -> p b t", t=2 * m)
                    if n >= 2:
                        dve.wait_ge(gl_level, GL * h + n - 1)
                    elif h:
                        dve.wait_ge(gl_kt_pe, h)
                    ref = blocks[:, :, at_:at_ + 1].to_broadcast([P, SEQ // (2 * m), 2 * m])
                    dve.tensor_tensor(e, blocks, ref, ALU.subtract).then_inc(gl_d, 1)

                def factors(n):
                    dve.wait_ge(gl_e, k_n + n + 1)
                    e = g_e[n % 2]
                    dve.tensor_tensor(g_qe[n % 2], q, e, ALU.mult)
                    dve.tensor_tensor(e, k, e, ALU.mult).then_inc(gl_f, 1)

                if part == 0:
                    dve.wait_ge(gl_b, h + 1)
                    difference(0)
                if 1 <= part <= 7:
                    factors(part - 1)
                    if part < 7:
                        difference(part)
                if part == 8:
                    dve.wait_ge(gl_level, GL * h + 6)
                    dve.wait_ge(gl_e, k_n + 8)
                    dve.tensor_tensor(g_qe[1], q, g_e[1], ALU.mult).then_inc(gl_f, 1)
                    difference(8)
                    dve.wait_ge(gl_e, k_n + 9)
                    dve.tensor_tensor(g_e[0], k, g_e[0], ALU.mult).then_inc(gl_f, 1)
                if part == 9:
                    dve.wait_ge(gl_level, GL * h + 2)
                    if h:
                        dve.wait_ge(gl_pv, h)
                    dve.memset(g_a, 0.0).then_inc(dve_step, 1)
                    dve.wait_ge(dve_step, chain.up())
                    dve.tensor_copy(g_a[0:64, :, 64:128], psum[0:64, 3, 0:256].rearrange("p (c t) -> p c t", c=NT))
                    for j in range(2):
                        ins = dve.tensor_copy(g_a[64 * j:64 * j + 32, :, 64 * j + 32:64 * j + 64],
                                              psum[64 * j:64 * j + 32, 3, 256:384].rearrange("p (c t) -> p c t", c=NT))
                    ins.then_inc(gl_a, 1)
                    dve.wait_ge(gl_level, GL * h + 8)
                    for i in range(6):
                        src = psum[:, 4 + i // 4, P * (i % 4):P * (i % 4) + P].rearrange("p (c t) -> p c t", c=NT)
                        m = g_mask[:, i:i + 1, :].to_broadcast([P, NT, 32])
                        ins = dve.tensor_tensor(g_small[:, i, :].rearrange("p (c t) -> p c t", c=NT), src, m, ALU.mult)
                    ins.then_inc(dve_step, 1)
                    dve.wait_ge(dve_step, chain.up())
                    for step in (3, 1, 1):
                        if step == 3:
                            dve.tensor_tensor(g_small[:, 0:3, :], g_small[:, 0:3, :], g_small[:, 3:6, :], ALU.add)\
                               .then_inc(dve_step, 1)
                            src = 1
                        else:
                            dve.tensor_tensor(g_small[:, 0, :], g_small[:, 0, :], g_small[:, src, :], ALU.add)\
                               .then_inc(dve_step, 1)
                            src += 1
                        dve.wait_ge(dve_step, chain.up())
                    for j in range(4):
                        s_ = slice(32 * j, 32 * j + 32)
                        ins = dve.tensor_copy(g_a[s_, :, s_], g_small[s_, 0, :].rearrange("p (c t) -> p c t", c=NT))
                    ins.then_inc(gl_a, 1)
                if part == 10:
                    for c in range(NT - 1):
                        dve.wait_ge(gl_upd, 3 * h + c + 1)
                        if c == 0:
                            dve.tensor_copy(g_state, psum[:, 2, 0:256]).then_inc(gl_state, 1)
                        else:
                            dve.wait_ge(gl_state, 3 * h + c)
                            dve.scalar_tensor_tensor(out=g_state, in0=g_state, scalar=g_last[:, c:c + 1],
                                                     in1=psum[:, 2, 0:256], op0=ALU.mult, op1=ALU.add).then_inc(gl_state, 1)
                if part == 11:
                    dve.wait_ge(gl_rstd, h + 1)
                    for i in range(2):
                        y = g_head[h % 2][i]
                        j = 2 * h + i
                        dve.scalar_tensor_tensor(out=y, in0=y, scalar=gain("gla_out_norm_g", i), in1=g_b,
                                                 op0=ALU.mult, op1=ALU.mult).then_inc(dve_step, 1)
                        dve.wait_ge(dve_step, chain.up())
                        dve.tensor_tensor(y, y, r[:, i, :], ALU.mult).then_inc(dve_step, 1)
                        dve.wait_ge(dve_step, chain.up())
                        dve.tensor_copy(uhi[:, j, :], y).then_inc(dve_step, 1)
                        dve.wait_ge(dve_step, chain.up())
                        dve.tensor_tensor(ulo[:, j, :], y, uhi[:, j, :].bitcast(F32), ALU.subtract).then_inc(gl_out, 1)

            def bias(half, i):
                if i < 0:
                    dve.wait_ge(sink_in, 16)
                    dve.tensor_scalar(sinks_neg, sinks, -1.0, None, ALU.mult).then_inc(dve_step, 1)
                    dve.wait_ge(dve_step, chain.up())
                    dve.wait_ge(rpb_turned, 1)
                    for half in range(2):
                        src = psum[0:31, 5, 0:120].rearrange("p (h j) -> p h j", h=8)[:, :, 1 - half:15 - half]
                        dve.tensor_copy(rpb_cols[32 * half:32 * half + 31, :].rearrange("p (h j) -> p h j", h=8), src)\
                           .then_inc(rpb_ready, 1)

            PARTS = {"ret": ret, "att": att, "heads_out": heads_out, "bias": bias, "lg": lg, "gla": gla, "mask": mask}

            def static(name):
                if name == "l3":
                    rates()
                for u, prev, parts in steps[name]:
                    if u is not None:
                        split_lo(u + 2, kt=units[u + 2][4])
                    if prev is not None:
                        post(prev)
                    for part in parts:
                        PARTS[part[0]](*part[1:])

            def norm(n):
                _, name, k0 = NORMS[n]
                dve.wait_ge(norm_rstd, n + 1)
                for k in range(KD):
                    dve.scalar_tensor_tensor(out=hn[:, k, :], in0=x[:, k, :], scalar=gain(name, k0 + k),
                                             in1=tmp[:, 1, :], op0=ALU.mult, op1=ALU.mult).then_inc(norm_h, 1)
                for k in range(KD):
                    dve.wait_ge(norm_hi, KD * n + k + 1)
                    dve.tensor_tensor(hlo[:, k, :], hn[:, k, :], hhi[:, k, :].bitcast(F32), ALU.subtract).then_inc(norm_lo, 1)

            def ff_block(b, more, last=False):
                for j in range(16):
                    if not (last and j >= 14):
                        split_lo(b + j + 2, more)
                    if j:
                        post(b + j - 1, more)
                post(b + 15, more)

            def ff(i):
                b = steps[f"ff{i}"]
                with dve.Fori(0, FB - (i == 2)) as f:
                    chain.loop = f * 16
                    n0 = chain.n
                    ff_block(b, f * 16)
                    assert chain.n == n0 + 16
                chain.n += 16 * (FB - (i == 2) - 1)
                chain.loop = 0
                if i == 2:
                    ff_block(b, 16 * (FB - 1), last=True)

            dve.wait_ge(const_done, CONSTS)
            split_lo(0)
            split_lo(1)
            dve.wait_ge(x_turned, KD + 1)
            dve.tensor_copy(vec[:, 0:VALL], MB[:, 0:VALL]).then_inc(vec_ready, 1)
            dve.wait_ge(vec_ready, 1)
            b0 = VEC["branch_gate_bias"][0]
            dve.tensor_scalar(nbias[:, :], vec[:, b0:b0 + 16], -1.0, None, ALU.mult).then_inc(vec_ready, 1)
            for n, (name, _, _) in enumerate(NORMS):
                norm(n)
                if name.startswith("ff"):
                    ff(int(name[2]))
                else:
                    static(name)

        @block.tensor
        def _(pe):
            def products(u, n0, n1, hi, lo, more=0):
                kt = units[u][4]
                g = psum[:, u % 2, :]
                for n in range(n0, n1):
                    k, part = divmod(n, 3)
                    w, v = ((whi, hi), (whi, lo), (wlo, hi))[part]
                    mm = pe.matmul(g, w[:, u % 4, k, :], v[:, k, :], start=n == 0, stop=n == 3 * kt - 1)
                if n1 == 3 * kt:
                    mm.then_inc(unit_done, 1)

            def begin(u, more=0):
                pe.wait_ge(lo_done, u + 1 + more)
                if u >= 2:
                    pe.wait_ge(evacuated, u - 1 + more)

            def shared_bank(u):
                if u not in shared_before:
                    return
                pe.wait_ge(evacuated, u + 1)
                if shared_before[u] is not None:
                    pe.wait_ge(posted, shared_before[u] + 1)
                if units[u][0] == "turn":
                    for t in range(NT):
                        mm = pe.transpose(XB[:, P * t:P * t + P], stage[:, u % 2, P * t:P * t + P], ident[:, :])
                    mm.then_inc(turned, 1)
                else:
                    pe.matmul(XB, bones[:, :], tmp[:, u % 2, :], start=True, stop=True).then_inc(head_sum, 1)

            def ret(h, part):
                q, k, v = r_q[h % 2], r_k[h % 2], r_v[h % 2]
                if part < 2:
                    for j in (2 * part, 2 * part + 1):
                        if j == 0:
                            pe.wait_ge(posted, UNIT_OF["silu", "w_in_o_2", 0, 4 * D + 2 * P * h + P] + 1)
                        if NT * h + j >= 2:
                            pe.wait_ge(ret_a, NT * h + j - 1)
                        pe.matmul(psum[:, 2 + j % 2, :], k[:, P * j:P * j + P], q, start=True, stop=True).then_inc(ret_qk, 1)
                if part == 2:
                    if h:
                        pe.wait_ge(ret_y, 2 * h)
                    for j in range(NT):
                        pe.wait_ge(ret_a, NT * h + j + 1)
                        for i in range(2):
                            mm = pe.matmul(psum[:, 4 + i, :], v[:, j, P * i:P * i + P], r_a[:, j, :],
                                           start=j == 0, stop=j == NT - 1)
                    mm.then_inc(ret_pv, 1)
                if part in (3, 4):
                    if part == 3:
                        pe.wait_ge(ret_y, 2 * h + 2)
                        if h:
                            pe.wait_ge(ret_rstd, h)
                    else:
                        pe.wait_ge(ret_sq, h + 1)
                    src = r_y if part == 3 else r_sq
                    for i in range(2):
                        mm = pe.matmul(MB, ones[:, :], src[:, i, :], start=i == 0, stop=i == 1)
                    mm.then_inc(ret_mean if part == 3 else ret_var, 1)

            def att(run, s, k=0):
                at, count = run_at[run], run_n[run]
                turn_lag, use_lag = ATT[run]

                def scores():
                    g = at + s
                    it = items[g]
                    pe.wait_ge(posted, it["unit"] + 1)
                    back = 3 if run != "dil" else 1
                    if s == 0:
                        if g:
                            pe.wait_ge(att_o, g)
                        if run == "dil":
                            pe.wait_ge(mask_copied, 1)
                        else:
                            pe.wait_ge(near_made, {"win": 8, "near": 16}[run])
                    elif s >= back:
                        pe.wait_ge(att_sm, g - back + 1)
                    for _, b, q, k, _ in it["segments"]:
                        mm = pe.matmul(psum[:, 2 + b, 0:k.shape[1]], q, k, start=True, stop=True)
                    mm.then_inc(att_qk, 1)

                def use(g):
                    it = items[g]
                    pt = it["pt"][g % len(it["pt"])]
                    pe.wait_ge(att_copy, rounds[g + 1])
                    if g:
                        pe.wait_ge(att_o, g)
                    n = len(it["values"])
                    for b in range(n):
                        mm = pe.matmul(MB[:, 0:E], pt[:, P * b:P * b + P], it["values"][b], start=b == 0, stop=b == n - 1)
                    mm.then_inc(att_pv, 1)

                def turn(g, only=None):
                    it = items[g]
                    p = it["p"][g % len(it["p"])]
                    pe.wait_ge(att_exp, g + 1)
                    n = len(it["values"])
                    for r in range(-(-n // 4)):
                        if only is not None and r != only:
                            continue
                        if rounds[g] + r:
                            pe.wait_ge(att_copy, rounds[g] + r)
                        for b in range(4 * r, min(4 * r + 4, n)):
                            mm = pe.transpose(psum[:, 5, P * (b % 4):P * (b % 4) + P], p[:, P * b:P * b + P], ident[:, :])
                        mm.then_inc(att_t, 1)

                if run == "dil":
                    if k == 0 and 0 <= s - use_lag < count:
                        use(at + s - use_lag)
                    if k == 0 and s < count:
                        scores()
                    if k and 0 <= s - turn_lag < count:
                        turn(at + s - turn_lag, k - 1)
                    return
                if s < count:
                    scores()
                if 0 <= s - use_lag < count:
                    use(at + s - use_lag)
                if 0 <= s - turn_lag < count:
                    turn(at + s - turn_lag)

            def heads_out(half, i):
                n = max(4 * half, 0) + i
                m = out_index(half, i)
                first_layer = half < 0
                if i == 0:
                    if first_layer:
                        pe.wait_ge(att_o, 32)
                    else:
                        pe.wait_ge(att_o, run_at["near"] + (32 if half else 0))
                if i >= 2 or half == 1:
                    pe.wait_ge(out_lo, m - 1)
                src = d_heads if first_layer else heads
                for t in range(NT):
                    mm = pe.transpose(psum[:, 2 + n % 2, P * t:P * t + P], src[:, t, P * i:P * i + P], ident[:, :])
                mm.then_inc(out_pe, 1)

            def mask():
                pe.wait_ge(pick_ready, 1)
                for i, m in enumerate((4, 16)):
                    mm = pe.matmul(psum[:, 2, P * i:P * i + P], d_pick[0:m, i, :], d_pick[0:m, i, :], start=True, stop=True)
                mm.then_inc(mask_sums, 1)

            def lg(t):
                if t == 0:
                    pe.wait_ge(up_in, 32)
                    pe.wait_ge(posted, UNIT_OF["copy", "w_in", 0, PA] + 1)
                    pe.wait_ge(out_lo, 4)
                pe.matmul(psum[:, 2 + t, :], g_pa[0:17, P * t:P * t + P], g_up[0:17, :], start=True, stop=True).then_inc(lg_pe, 1)

            def gla(h, part):
                q, k, v, r = g_head[h % 2]

                def level(n):
                    if n < 7:
                        pe.wait_ge(gl_f, 9 * h + n + 1)
                        ke, qe = g_e[n % 2], g_qe[n % 2]
                    else:
                        ke, qe = k, q
                    if n == 0:
                        for c in range(NT):
                            mm = pe.matmul(psum[0:64, 3, 64 * c:64 * c + 64], ke[:, P * c:P * c + 64],
                                           qe[:, P * c + 64:P * c + P], start=True, stop=True)
                    elif n == 1:
                        for c in range(NT):
                            for j in range(2):
                                o = P * c + 64 * j
                                mm = pe.matmul(psum[64 * j:64 * j + 32, 3, 256 + 32 * c:288 + 32 * c], ke[:, o:o + 32],
                                               qe[:, o + 32:o + 64], start=True, stop=True)
                    else:
                        i = n - 2
                        for c in range(NT):
                            for j in range(4):
                                o = P * c + 32 * j
                                at_ = P * (i % 4) + 32 * c
                                mm = pe.matmul(psum[32 * j:32 * j + 32, 4 + i // 4, at_:at_ + 32], ke[:, o:o + 32],
                                               qe[:, o:o + 32], start=True, stop=True)
                    mm.then_inc(gl_level, 1)

                if part == 0:
                    pe.wait_ge(posted, UNIT_OF["silu", "w_in", 0, RG + 2 * P * h + P] + 1)
                    if h == 0:
                        pe.wait_ge(lg_done, NT)
                    else:
                        pe.wait_ge(gl_state, 3 * h)
                    for c in range(NT):
                        mm = pe.matmul(psum[:, 2, P * c:P * c + P], g_lg[:, c, P * h:P * h + P], tri[:, :], start=True, stop=True)
                    mm.then_inc(gl_b_pe, 1)
                if part == 2:
                    if h:
                        pe.wait_ge(gl_kt, h)
                        pe.wait_ge(gl_o, 2 * h)
                if 2 <= part <= 8:
                    level(part - 2)
                if part == 8:
                    level(7)
                if part == 9:
                    pe.wait_ge(gl_f, 9 * h + 9)
                    pe.wait_ge(gl_a, 2 * h + 1)
                    for c in range(NT):
                        mm = pe.transpose(psum[:, 3, P * c:P * c + P], g_e[0][:, P * c:P * c + P], ident[:, :])
                    mm.then_inc(gl_kt_pe, 1)
                if part == 10:
                    pe.wait_ge(gl_a, 2 * h + 2)
                    pe.wait_ge(gl_kt, h + 1)
                    for c in range(NT):
                        if c:
                            pe.wait_ge(gl_state, 3 * h + c)
                        for i in range(2):
                            o = psum[:, 4 + i, P * c:P * c + P]
                            mm = pe.matmul(o, v[:, c, P * i:P * i + P], g_a[:, c, :], start=True, stop=c == 0)
                            if c:
                                mm = pe.matmul(o, g_state[:, P * i:P * i + P], g_qe[1][:, P * c:P * c + P], start=False, stop=True)
                        if c < NT - 1:
                            pe.matmul(psum[:, 2, 0:256], g_kt[:, c, :], v[:, c, :], start=True, stop=True).then_inc(gl_upd, 1)
                    mm.then_inc(gl_pv, 1)
                if part == 11:
                    for i in range(2):
                        pe.wait_ge(gl_sq, 2 * h + i + 1)
                        mm = pe.matmul(MB, ones[:, :], g_qe[i], start=i == 0, stop=i == 1)
                    mm.then_inc(gl_sum, 1)

            def bias(half, i):
                if i < 0:
                    pe.wait_ge(rpb_in, 16)
                    pe.transpose(psum[0:31, 5, 0:120], rpb_rows[0:120, :], ident[0:120, 0:120]).then_inc(rpb_turned, 1)
                    return
                if i == 0:
                    pe.wait_ge(rpb_ready, 2)
                    pe.wait_ge(dist_pool, 1)
                    if half:
                        pe.wait_ge(out_lo, OUT0 + 4)
                if i >= 2:
                    pe.wait_ge(near_made, 8 * half + i - 1)
                for c in range(8):
                    z = 63 - (8 * i + c)
                    for low in range(2):
                        r = slice(32 * low, 32 * low + 31)
                        mm = pe.matmul(psum[64 * low:64 * low + 64, 2 + i % 2, 56 * c:56 * c + 56], select[r, z:z + 64],
                                       rpb_cols[r, 56 * half:56 * half + 56], start=True, stop=True)
                mm.then_inc(near_sums, 1)

            PARTS = {"ret": ret, "att": att, "heads_out": heads_out, "bias": bias, "lg": lg, "gla": gla, "mask": mask}
            MIXED = {}
            if "l1" in steps:
                MIXED["l1", UNIT_OF["branch", "w_attn_branch", 0, 0]] = lambda: pe.wait_ge(out_lo, 4)
                MIXED["l1", UNIT_OF["branch", "w_gla_branch", 0, 0]] = lambda: pe.wait_ge(gl_out, 8)
                MIXED["l1", UNIT_OF["mix", "w_out", 0, 0]] = lambda: pe.wait_ge(posted, UNIT_OF["mix", "w_out", 0, 0])
            if "l2" in steps:
                MIXED["l2", UNIT_OF["down", "w_out_e_2", 0, 0]] = lambda: pe.wait_ge(out_lo, OUT0 + 4)
                MIXED["l2", UNIT_OF["down", "w_out_e_2", 512, 0]] = lambda: pe.wait_ge(out_lo, OUT0 + 8)
            if "l3" in steps:
                MIXED["l3", UNIT_OF["down", "w_out_o_2", 0, 0]] = lambda: pe.wait_ge(ret_out, 8)
                MIXED["l3", UNIT_OF["down", "w_out_o_2", D, 0]] = lambda: pe.wait_ge(ret_out, 16)

            def static(name):
                start = first(name)
                for u, prev, parts in steps[name]:
                    if u is not None:
                        begin(u)
                        if u == start:
                            pe.wait_ge(norm_lo, KD * (ORDER[name] + 1))
                        total = 3 * units[u][4]
                        operand = (uhi, ulo) if units[u][0] in ("down", "branch") else (hhi, hlo)
                        if units[u][0] in ("down", "branch") and units[u][4] == 4 and units[u][2]:
                            operand = uhi[:, 4:8, :], ulo[:, 4:8, :]
                        if (name, u) in MIXED:
                            MIXED[name, u]()
                    todo = [lambda: shared_bank(prev)] * (prev is not None) + [(lambda part=part: PARTS[part[0]](*part[1:])) for part in parts]
                    for i, part in enumerate(todo):
                        if u is not None:
                            n = len(todo) + 1
                            products(u, total * i // n, total * (i + 1) // n, *operand)
                        part()
                    if u is not None:
                        products(u, total * len(todo) // (len(todo) + 1), total, *operand)

            def norm(n):
                for k in range(KD):
                    pe.wait_ge(norm_sq, KD * n + k + 1)
                    pe.matmul(MB, ones[:, :], tmp[:, k % 2, :], start=k == 0, stop=k == KD - 1).then_inc(norm_sum, 1)

            def ff(i):
                b = steps[f"ff{i}"]
                with pe.Fori(0, FB) as f:
                    for j in range(16):
                        u = b + j
                        begin(u, f * 16)
                        if j == 0:
                            pe.wait_ge(norm_lo, KD * (ORDER[f"ff{i}"] + 1))
                        for k in range(KD):
                            if j == 8:
                                pe.wait_ge(posted, b + k + 1 + f * 16)
                            products(u, 3 * k, 3 * k + 3, *((hhi, hlo) if j < 8 else (uhi, ulo)))

            pe.wait_ge(const_done, CONSTS)
            pe.wait_ge(x_in, 16)
            for k in range(KD):
                if k >= 2:
                    pe.wait_ge(x_ready, k - 1)
                for t in range(NT):
                    mm = pe.transpose(psum[:, k % 2, P * t:P * t + P], xin[:, t, P * k:P * k + P], ident[:, :])
                mm.then_inc(x_turned, 1)
            pe.wait_ge(vec_in, 16 * (len(VEC) + 2 * len(HEADVEC)))
            pe.transpose(MB[:, 0:VALL], rows[0:VALL, :], ident[0:VALL, 0:VALL]).then_inc(x_turned, 1)
            pe.wait_ge(x_ready, KD)
            pe.wait_ge(vec_ready, 1)
            for n, (name, _, _) in enumerate(NORMS):
                norm(n)
                if name.startswith("ff"):
                    ff(int(name[2]))
                else:
                    static(name)
            pe.wait_ge(posted, len(units))
            for n in range(2 * NT):
                if n >= 2:
                    pe.wait_ge(out_copied, n - 1)
                for k in range(4):
                    mm = pe.transpose(psum[:, n % 2, P * k:P * k + P],
                                      x[:, 4 * (n % 2) + k, P * (n // 2):P * (n // 2) + P], ident[:, :])
                mm.then_inc(out_turned, 1)


def kernel(**inputs):
    import numpy as _np
    import concourse.bacc as _bacc
    from concourse.bass_utils import run_bass_kernel_spmd as _run

    nc = _bacc.Bacc("TRN2", target_bir_lowering=False, num_devices=1)
    arrays, args = {}, {}
    for name, value in inputs.items():
        v = _np.ascontiguousarray(value)
        arrays[f"in_{name}_dram"] = v
        args[name] = nc.dram_tensor(f"in_{name}_dram", v.shape, mybir.dt.from_np(v.dtype), kind="ExternalInput").ap()
    out = nc.dram_tensor("out_0_dram", (1, SEQ, D), F32, kind="ExternalOutput").ap()
    build(nc, args, out)
    r = _run(nc, [arrays], core_ids=[0])
    return r.results[0]["out_0_dram"]
```

```python
from contextlib import ExitStack

import concourse.bass as bass
from concourse import mybir

F32 = mybir.dt.float32
F32R = mybir.dt.float32r
ALU = mybir.AluOpType
ACT = mybir.ActivationFunctionType
AX = mybir.AxisListType

P = 128
SEQ = 512
D = 1024
KD = D // P
NT = SEQ // P
FF = 4 * D
FB = FF // D
EPS = 1e-6
GN_EPS = 1e-5
NEG = -1.0e30

E = 64
QKV = 3 * 24 * E
QG, KG, VG = QKV, QKV + 512, QKV + 1024
RG, PA, GATE = QKV + 2048, QKV + 3072, QKV + 3088
GROUPS = 3
QA, KA, VA, QB, KB, VB = 0, 512, 640, 768, 1280, 1792
HEADS = 8

VEC = {}
for name, tiles in (("norm1_g", 8), ("norm2_g", 8), ("attn_norm_e_2", 8), ("ret_norm_o_2", 8), ("mlp_norm_2", 16),
                    ("gla_out_norm_g", 2), ("branch_gate_bias", 16), ("ret_gn_o_2", 16)):
    VEC[name] = sum(n for _, n in VEC.values()), tiles
VROWS = sum(n for _, n in VEC.values())
HEADVEC = ["attn_q_norm_g", "attn_k_norm_g", "q_norm_a_2", "k_norm_a_2", "q_norm_b_2", "k_norm_b_2"]
VALL = VROWS + len(HEADVEC)

WEIGHTS = ["w_in", "w_attn_branch", "w_gla_branch", "w_out", "w_ff_up", "w_ff_down", "w_in_e_2", "w_out_e_2",
           "w_in_o_2", "w_out_o_2", "w_mlp_in_2", "w_mlp_out_2"]




class Count:

    def __init__(self):
        self.n = 0
        self.loop = 0

    def up(self):
        self.n += 1
        return self.n + self.loop


def plan():
    units = []
    steps = {}

    def pipeline(name, todo):
        out = steps.setdefault(name, [])
        prev = None
        for spec, part in todo:
            part = part if isinstance(part, list) else [part] if part else []
            if spec is not None:
                units.append(spec)
                out.append((len(units) - 1, prev, part))
                prev = len(units) - 1
            else:
                out.append((None, prev, part))
                prev = None
        if prev is not None:
            out.append((None, prev, []))

    def ff(i, w1, w2, row):
        steps[f"ff{i}"] = len(units)
        for f in range(FB):
            for j in range(KD):
                units.append(("up", w1, row, f * D + P * j, KD, j))
            for j in range(KD):
                units.append(("down", w2, row * 4 + f * D, P * j, KD, j))

    def beside(specs, parts):
        n = len(specs)
        return [(s, parts[len(parts) * i // n:len(parts) * (i + 1) // n]) for i, s in enumerate(specs)]

    w = "w_in"
    dil = [[("att", "dil", s, k) for k in range(4)] for s in range(32 + ATT["dil"][1])]

    def three(p):
        return ([("head", w, 0, 512 * g + P * p, KD, ("d", "q", p, g)) for g in range(GROUPS)]
                + [("head", w, 0, 1536 + 512 * g + P * p, KD, ("d", "k", p, g)) for g in range(GROUPS)]
                + [("turn", w, 0, 3072 + 512 * g + P * p, KD, ("d", p, g)) for g in range(GROUPS)])

    def gates(branch):
        return [("sigmoid", w, 0, GATE + D * branch + P * j, KD, (branch, j)) for j in range(KD)]

    def gla_head(h):
        return ([("copy", w, 0, QG + P * h, KD, ("gq", h)), ("copy", w, 0, KG + P * h, KD, ("gk", h))]
                + [("turn", w, 0, VG + 2 * P * h + P * i, KD, ("g", h, i)) for i in range(2)]
                + [("silu", w, 0, RG + 2 * P * h + P * i, KD, ("g", h, i)) for i in range(2)])

    todo = [(s, [("mask",)] if i == 1 else None) for i, s in enumerate(three(0))]
    for p in range(1, 4):
        q = dil[8 * (p - 1):8 * p]
        todo += zip(three(p), [q[0] + q[1]] + q[2:] + [None, None])
    q = dil[24:]
    todo += zip(gates(0), [q[0] + q[1]] + q[2:8] + [q[8] + q[9]])
    todo += [(("copy", w, 0, PA, KD, ("pa", 0)), [("heads_out", -1, i) for i in range(4)])]
    gla = [[[("gla", h, i), ("gla", h, i + 1)] for i in range(0, 12, 2)] for h in range(4)]
    todo += zip([("branch", "w_attn_branch", 0, P * j, 4, (0, j)) for j in range(KD)],
                [None, ("lg", 0), None, ("lg", 1), None, ("lg", 2), None, ("lg", 3)])
    todo += [(s, None) for s in gla_head(0)]
    for h in range(1, 4):
        todo += zip(gla_head(h), gla[h - 1])
    todo += zip(gates(1), gla[3] + [None, None])
    todo += [(("branch", "w_gla_branch", 0, P * j, KD, (1, j)), None) for j in range(KD)]
    todo += [(("mix", "w_out", 0, P * j, KD, j), None) for j in range(KD)]
    pipeline("l1", todo)
    ff(0, "w_ff_up", "w_ff_down", 0)

    w = "w_in_e_2"

    def pair(p):
        return [("head", w, 0, QB + P * p, KD, ("b", "q", p)), ("head", w, 0, KB + P * p, KD, ("b", "k", p)),
                ("turn", w, 0, VB + P * p, KD, ("b", p))]

    def w_out_e(half):
        return [("down", "w_out_e_2", 512 * half, P * j, 4, j) for j in range(KD)]

    specs = ([("head", w, 0, QA + P * i, KD, ("a", "q", i)) for i in range(4)]
             + [("head", w, 0, KA, KD, ("a", "k", 0)), ("turn", w, 0, VA, KD, ("a", 0))])
    todo = [(specs[0], None)] + beside(specs[1:], [("bias", 0, i) for i in range(-1, 8)])
    todo += beside(pair(0) + pair(1), [("att", "win", i) for i in range(32 + ATT["win"][1])])
    todo += [(None, [("heads_out", 0, i)]) for i in range(4)]
    near = [("att", "near", i) for i in range(32 + ATT["near"][1])]
    todo += beside(w_out_e(0)[:4], [("bias", 1, i) for i in range(8)] + near[0:8])
    for p in (2, 3):
        n = 8 * (p - 1)
        todo += list(zip(pair(p), (near[n:n + 3], near[n + 3:n + 6], near[n + 6:n + 8])))
    todo += beside(w_out_e(0)[4:], near[24:])
    todo += [(None, [("heads_out", 1, i)]) for i in range(4)]
    todo += [(s, None) for s in w_out_e(1)]
    pipeline("l2", todo)
    ff(1, "w_mlp_in_2", "w_mlp_out_2", 0)

    def head(h):
        w = "w_in_o_2"
        return ([("copy", w, 0, P * h, KD, ("q", h)), ("copy", w, 0, D + P * h, KD, ("k", h))]
                + [("turn", w, 0, 2 * D + 2 * P * h + P * i, KD, (h, i)) for i in range(2)]
                + [("silu", w, 0, 4 * D + 2 * P * h + P * i, KD, (h, i)) for i in range(2)])

    ret = [[("ret", h, i) for i in range(6)] for h in range(HEADS)]
    todo = [(s, None) for s in head(0)]
    for h in range(1, 5):
        todo += zip(head(h), ret[h - 1])
    todo += zip([("down", "w_out_o_2", 0, P * j, KD, j) for j in range(KD)], ret[4][:4] + [None] * 4)
    todo += zip(head(5), ret[4][4:] + [None] * 4)
    todo += zip(head(6), ret[5])
    todo += zip(head(7), ret[6])
    todo += zip([("down", "w_out_o_2", D, P * j, 4, j) for j in range(KD)], ret[7] + [None] * 2)
    todo += [(("down", "w_out_o_2", D + 4 * P, P * j, 4, j), None) for j in range(KD)]
    pipeline("l3", todo)
    ff(2, "w_mlp_in_2", "w_mlp_out_2", D)
    return units, steps


ATT = {"win": (2, 3), "near": (2, 3), "dil": (1, 2)}


def build(nc, a, out):
    units, steps = plan()
    weights = {n: a[n].rearrange("a k n -> (a k) n") for n in WEIGHTS}
    with ExitStack() as ctx:
        def sb(name, shape, dt=F32):
            return ctx.enter_context(nc.sbuf_tensor(name, shape, dt))

        def sem(name):
            return ctx.enter_context(nc.semaphore(name))

        x = sb("x", [P, KD, SEQ])
        raw = sb("raw", [P, 4, KD, P])
        whi = sb("whi", [P, 4, KD, P], F32R)
        wlo = sb("wlo", [P, 4, KD, P], F32R)
        hhi = sb("hhi", [P, KD, SEQ], F32R)
        hlo = sb("hlo", [P, KD, SEQ], F32R)
        uhi = sb("uhi", [P, KD, SEQ], F32R)
        ulo = sb("ulo", [P, KD, SEQ], F32R)
        stage = sb("stage", [P, 2, SEQ])
        tmp = sb("tmp", [P, 2, SEQ])
        ident = sb("ident", [P, P])
        ones = sb("ones", [P, P])
        bones = sb("bones", [P, P])
        vec = sb("vec", [P, P])
        const = sb("const", [P, 4])
        squares = sb("squares", [P, SEQ])
        nbias = sb("nbias", [P, 16])
        arena = sb("arena", [P, 17000])
        psum = ctx.enter_context(nc.psum_tensor("psum", [P, 8, 512], F32))
        MB = psum[:, 7, :]
        eps = const[:, 0:1]

        def gain(name, k, tiles=0):
            c = VEC[name][0] + k
            return vec[:, c:c + 1]

        raw_in = [sem(f"raw_in{i}") for i in range(4)]
        hi_done, lo_done = sem("hi_done"), sem("lo_done")
        unit_done, evacuated, posted = sem("unit_done"), sem("evacuated"), sem("posted")
        x_in, vec_in = [sem(f"x_in{i}") for i in range(2)], sem("vec_in")
        const_done, x_turned = sem("const_done"), sem("x_turned")
        x_ready, vec_ready = sem("x_ready"), sem("vec_ready")
        dve_step, act_step = sem("dve_step"), sem("act_step")
        norm_sq, norm_sum, norm_total, norm_rstd = sem("norm_sq"), sem("norm_sum"), sem("norm_total"), sem("norm_rstd")
        norm_h, norm_hi, norm_lo = sem("norm_h"), sem("norm_hi"), sem("norm_lo")
        gate_ln, gate_log, gate_exp = sem("gate_ln"), sem("gate_log"), sem("gate_exp")
        out_turned, out_copied, out_done = sem("out_turned"), sem("out_copied"), sem("out_done")

        xin = arena[:, 0:NT * D].rearrange("p (t d) -> p t d", t=NT)
        rows = arena[:, 4096:4096 + P]
        hn = arena[:, 0:KD * SEQ].rearrange("p (k t) -> p k t", k=KD)
        xout = arena[:, 4096:4096 + NT * D].rearrange("p (t d) -> p t d", t=NT)

        NORMS = [("l1", "norm1_g", 0), ("ff0", "norm2_g", 0), ("l2", "attn_norm_e_2", 0), ("ff1", "mlp_norm_2", 0),
                 ("l3", "ret_norm_o_2", 0), ("ff2", "mlp_norm_2", KD)]
        ORDER = {n[0]: i for i, n in enumerate(NORMS)}

        def first(name):
            return steps[name] if name.startswith("ff") else steps[name][0][0]

        shared = [u for u, s in enumerate(units) if s[0] in ("turn", "head")]
        shared_before = {u: shared[i - 1] if i else None for i, u in enumerate(shared)}
        CONSTS = 8
        HALVINGS = (64, 32, 16, 8, 4, 2, 1)
        ARENA = 17000

        UNIT_OF = {s[:4]: u for u, s in enumerate(units)}
        XB = psum[:, 6, :]

        at = [0]

        def place(*shape):
            n = 1
            for d in shape:
                n *= d
            v = arena[:, at[0]:at[0] + n]
            at[0] += n
            assert at[0] <= ARENA, at[0]
            if len(shape) == 2:
                v = v.rearrange("p (a b) -> p a b", a=shape[0])
            return v

        r_q, r_k = [place(SEQ) for _ in range(2)], [place(SEQ) for _ in range(2)]
        r_v = [place(NT, 2 * P) for _ in range(2)]
        r_g = [place(2, SEQ) for _ in range(2)]
        r_dist, r_exp = place(7 * P), place(7 * P)
        r_decay = [place(7 * P) for _ in range(2)]
        r_a = place(NT, SEQ)
        r_y, r_sq = place(2, SEQ), place(2, SEQ)
        r_rstd = place(SEQ)
        r_lg, r_lt = place(16), place(16)
        rate_in, rate_ready, dist_ready = sem("rate_in"), sem("rate_ready"), sem("dist_ready")
        ret_exp, ret_decay, ret_qk, ret_a = sem("ret_exp"), sem("ret_decay"), sem("ret_qk"), sem("ret_a")
        ret_pv, ret_y, ret_mean, ret_yc = sem("ret_pv"), sem("ret_y"), sem("ret_mean"), sem("ret_yc")
        ret_sq, ret_var, ret_rstd, ret_out = sem("ret_sq"), sem("ret_var"), sem("ret_rstd"), sem("ret_out")
        turned, head_sum, head_rstd = sem("turned"), sem("head_sum"), sem("head_rstd")
        at[0] = 0
        d_q, d_k, d_v = [], [], []
        for _ in range(2):
            d_q.append(place(GROUPS, SEQ))
            d_k.append(place(GROUPS, SEQ))
            d_v.append(place(NT, GROUPS * P))
        d_bias = place(256 + 1024)
        d_p = [place(1280) for _ in range(2)]
        d_pt = [place(1280)]
        d_heads = place(NT, 8 * E)
        d_pick = place(2, P)
        at[0] = 0
        mixed = place(KD, SEQ)

        def gla_head_places():
            return place(SEQ), place(SEQ), place(NT, 2 * P), place(2, SEQ)

        gate1_at = at[0]
        g_head = [gla_head_places()]
        g_lg = place(NT, 4 * P)
        g_head.append(gla_head_places())
        g_b = place(SEQ)
        g_e, g_qe = [place(SEQ) for _ in range(2)], [place(SEQ) for _ in range(2)]
        g_a = place(NT, P)
        g_small = place(6, P)
        g_state, g_kt = place(2 * P), place(NT, P)
        g_states = [g_state, g_small[:, 0:2, :].rearrange("p a b -> p (a b)")]
        g_last = place(NT)
        gate1 = arena[:, gate1_at:gate1_at + KD * SEQ].rearrange("p (k t) -> p k t", k=KD)
        g_pa, g_up = g_kt.rearrange("p a b -> p (a b)"), g_a.rearrange("p a b -> p (a b)")
        tri = sb("tri", [P, P])
        g_mask = sb("g_mask", [P, 6, 32])
        pick_ready, mask_sums, mask_copied, mask_ready = (sem("pick_ready"), sem("mask_sums"), sem("mask_copied"),
                                                          sem("mask_ready"))
        up_in, pa_ones, lg_pe, lg_ln, lg_done = sem("up_in"), sem("pa_ones"), sem("lg_pe"), sem("lg_ln"), sem("lg_done")
        gl_b_pe, gl_b, gl_d, gl_e, gl_f = sem("gl_b_pe"), sem("gl_b"), sem("gl_d"), sem("gl_e"), sem("gl_f")
        gl_level, gl_a, gl_kt_pe, gl_kt = sem("gl_level"), sem("gl_a"), sem("gl_kt_pe"), sem("gl_kt")
        gl_upd, gl_state, gl_pv, gl_o = sem("gl_upd"), sem("gl_state"), sem("gl_pv"), sem("gl_o")
        gl_sq, gl_sum, gl_rstd, gl_out = sem("gl_sq"), sem("gl_sum"), sem("gl_rstd"), sem("gl_out")

        at[0] = 0
        e_q, e_k, e_k2, e_v = place(4, SEQ), place(SEQ), place(SEQ), place(NT, P)
        near_bias = [place(4 * 14 * 64), arena[:, 0:4 * 14 * 64]]
        n_q, n_k = [place(SEQ) for _ in range(2)], [place(SEQ) for _ in range(2)]
        n_v = [place(NT, P) for _ in range(2)]
        win_dist, win_bias = place(3 * P), [place(3 * P) for _ in range(2)]
        heads = place(NT, 8 * E)
        e_p = [place(SEQ) for _ in range(3)]
        e_pt = [place(SEQ) for _ in range(2)]
        rpb_rows, rpb_cols, select = place(31), place(8 * 14), place(192)
        sinks, sinks_neg = place(8), place(8)
        sink_in, rpb_in, near_made = sem("sink_in"), sem("rpb_in"), sem("near_made")
        near_masked, near_sums, win_ready, sel_ready = sem("near_masked"), sem("near_sums"), sem("win_ready"), sem("sel_ready")
        rpb_turned, rpb_ready, dist_pool, dist_abs = sem("rpb_turned"), sem("rpb_ready"), sem("dist_pool"), sem("dist_abs")
        win_made, sink_ready = sem("win_made"), sem("sink_ready")

        cols = sb("cols", [P, 4, 4])
        att_qk, att_sm, att_max, att_exp = sem("att_qk"), sem("att_sm"), sem("att_max"), sem("att_exp")
        att_t, att_copy, att_pv, att_o = sem("att_t"), sem("att_copy"), sem("att_pv"), sem("att_o")
        out_pe, out_hi, out_lo = sem("out_pe"), sem("out_hi"), sem("out_lo")

        items = []
        run_at = {}

        def unit_of(*key):
            return UNIT_OF[key]

        run_at["dil"] = len(items)
        for h in range(HEADS):
            r = slice(64 * (h % 2), 64 * (h % 2) + 64)
            buf = (h // 2) % 2
            for n in range(NT):
                segments, values, c0 = [], [], 0
                for g in range(GROUPS):
                    lo = max(n - 1, 0) if g == 0 else 0
                    w = (n + 1 - lo) * P
                    end = 256 if g == 0 else 256 + 512 * g
                    segments.append((c0, g, d_q[buf][r, g, P * n:P * n + P], d_k[buf][r, g, P * lo:P * (n + 1)],
                                     d_bias[:, end - w:end]))
                    values += [d_v[buf][:, b, P * g + E * (h % 2):P * g + E * (h % 2) + E] for b in range(lo, n + 1)]
                    c0 += w
                items.append(dict(run="dil", h=h, width=c0, scale=E ** -0.5, segments=segments, values=values, sink=None,
                                  out=d_heads[:, n, E * h:E * h + E], unit=UNIT_OF["turn", "w_in", 0, 4096 + P * (h // 2)]))
        run_at["win"] = len(items)
        for h in range(HEADS):
            r = slice(64 * (h % 2), 64 * (h % 2) + 64)
            keys = e_k if h // 4 == h % 2 else e_k2
            for n in range(NT):
                lo, hi = max(n - 1, 0), min(n + 2, NT)
                items.append(dict(
                    run="win", h=h, width=(hi - lo) * P, scale=E ** -0.5,
                    segments=[(0, len(items) % 3, e_q[r, h // 2, P * n:P * n + P], keys[r, P * lo:P * hi],
                               win_bias[h % 2][:, P * (lo - n + 1):P * (hi - n + 1)])],
                    values=[e_v[:, b, E * (h // 4):E * (h // 4) + E] for b in range(lo, hi)], sink=h,
                    out=heads[:, n, E * h:E * h + E], unit=UNIT_OF["turn", "w_in_e_2", 0, VA]))
        run_at["near"] = len(items)
        for h in range(HEADS):
            r = slice(64 * (h % 2), 64 * (h % 2) + 64)
            p = h // 2
            for n in range(NT):
                j = (h % 4) * 14 + 6 - 2 * n
                items.append(dict(
                    run="near", h=h, width=SEQ, scale=E ** -0.5,
                    segments=[(0, len(items) % 3, n_q[p % 2][r, P * n:P * n + P], n_k[p % 2][r, :],
                               near_bias[h // 4][:, 64 * j:64 * (j + 8)])],
                    values=[n_v[p % 2][:, b, E * (h % 2):E * (h % 2) + E] for b in range(NT)], sink=None,
                    out=heads[:, n, E * h:E * h + E], unit=UNIT_OF["turn", "w_in_e_2", 0, VB + P * p]))
        run_n = {r: sum(it["run"] == r for it in items) for r in run_at}
        rounds = [0]
        for it in items:
            rounds.append(rounds[-1] + -(-len(it["values"]) // 4))
            it["p"] = e_p if it["run"] != "dil" else d_p
            it["pt"] = e_pt if it["run"] != "dil" else d_pt
        GL = 8
        OUT0 = 4

        def out_index(half, i):
            return i if half < 0 else OUT0 + 4 * half + i

        TURNS = {u: i for i, u in enumerate(u for u, s in enumerate(units) if s[0] == "turn")}
        HEADU = {u: i for i, u in enumerate(u for u, s in enumerate(units) if s[0] == "head")}

        GATES = ("silu", "sigmoid")
        GATEU = {u: i for i, u in enumerate(u for u, s in enumerate(units) if s[0] in GATES)}

        block = ctx.enter_context(nc.Block())

        @block.sync
        def _(sp):
            for i in range(2):
                c = slice(512 * i, 512 * i + 512)
                sp.dma_start(xin[:, :, c], a["x"][0].rearrange("(t p) d -> p t d", p=P)[:, :, c]).then_inc(x_in[i], 16)

            def load(u, row=0, col=0, more=0):
                _, name, row0, col0, kt, _ = units[u]
                if u >= 4:
                    sp.wait_ge(hi_done, u - 3 + more)
                    sp.wait_ge(lo_done, u - 3 + more)
                src = weights[name][bass.ds(row0 + row, kt * P), bass.ds(col0 + col, P)]
                sp.dma_start(raw[:, u % 4, 0:kt, :], src.rearrange("(k p) c -> p k c", p=P)).then_inc(raw_in[u % 4], 16)

            def static(name):
                for u, _, _ in steps[name]:
                    if u is not None and u >= 4:
                        load(u)

            def ff(i):
                with sp.Fori(0, FB) as f:
                    for j in range(16):
                        load(steps[f"ff{i}"] + j, 0 if j < 8 else f * D, f * D if j < 8 else 0, f * 16)

            for u in range(4):
                load(u)
            for name, (r0, n) in VEC.items():
                sp.dma_start(rows[r0:r0 + n, :], a[name].rearrange("a (n p) -> (a n) p", p=P)).then_inc(vec_in, 16)
            for i, name in enumerate(HEADVEC):
                for half in range(2):
                    sp.dma_start(rows[VROWS + i:VROWS + i + 1, 64 * half:64 * half + 64], a[name]).then_inc(vec_in, 16)
            for name, _, _ in NORMS:
                if name.startswith("ff"):
                    ff(int(name[2]))
                else:
                    static(name)
            for t in range(NT):
                sp.wait_ge(out_copied, 2 * t + 2)
                sp.dma_start(out[0, P * t:P * t + P, :], xout[:, t, :]).then_inc(out_done, 16)
            sp.wait_ge(out_done, 16 * NT)

        @block.gpsimd
        def _(pool):
            count = Count()

            def done(ins):
                ins.then_inc(const_done, 1)
                pool.wait_ge(const_done, count.up())

            done(pool.memset(ones[:, :], 1.0))
            done(pool.memset(const[:, 0:1], EPS))
            done(pool.memset(const[:, 1:2], GN_EPS))
            done(pool.memset(bones[:, :], 0.0))
            for i in range(2):
                done(pool.memset(bones[64 * i:64 * i + 64, 64 * i:64 * i + 64], 1.0))
            done(pool.memset(ident[:, :], 0.0))
            done(pool.affine_select(out=ident[:, :], in_=ident[:, :], compare_op=ALU.not_equal, fill=1.0, base=0,
                                    pattern=[[-1, P]], channel_multiplier=1))
            done(pool.memset(tri[:, :], 1.0))
            done(pool.affine_select(out=tri[:, :], in_=tri[:, :], compare_op=ALU.is_ge, fill=0.0, base=0,
                                    pattern=[[1, P]], channel_multiplier=-1))
            done(pool.memset(g_mask[:, :, :], 0.0))
            for i, m in enumerate(HALVINGS[2:]):
                v = g_mask[:, i, :].rearrange("p (b h w) -> p b h w", h=2, w=m)[:, :, 1, :]
                done(pool.memset(v, 1.0))
                for j in range(4):
                    r = v[32 * j:32 * j + 32]
                    done(pool.affine_select(out=r, in_=r, compare_op=ALU.is_ge, fill=0.0, base=0,
                                            pattern=[[-2 * m, 16 // m], [0, m]], channel_multiplier=1))
                    done(pool.affine_select(out=r, in_=r, compare_op=ALU.is_ge, fill=0.0, base=m - 1,
                                            pattern=[[2 * m, 16 // m], [0, m]], channel_multiplier=-1))
            for j in range(4):
                r = g_mask[32 * j:32 * j + 32, 5, :]
                done(pool.affine_select(out=r, in_=r, compare_op=ALU.not_equal, fill=1.0, base=0,
                                        pattern=[[-1, 32]], channel_multiplier=1))
            pool.wait_ge(norm_lo, KD)
            done(pool.memset(d_pick, 0.0))
            for i, m in enumerate((4, 16)):
                v = d_pick[0:m, i, :].rearrange("p (a b) -> p a b", b=m)
                done(pool.affine_select(out=v, in_=v, compare_op=ALU.not_equal, fill=1.0, base=0,
                                        pattern=[[0, P // m], [-1, m]], channel_multiplier=1))
            pool.sem_inc(pick_ready, 1)
            pool.wait_ge(mask_copied, 1)
            v = d_bias[:, 0:P]
            done(pool.affine_select(out=v, in_=v, compare_op=ALU.is_ge, fill=NEG, base=0, pattern=[[1, P]],
                                    channel_multiplier=-1))
            for c in (P, 256 + 3 * P, 256 + 7 * P):
                v = d_bias[:, c:c + P]
                done(pool.affine_select(out=v, in_=v, compare_op=ALU.is_ge, fill=NEG, base=0, pattern=[[-1, P]],
                                        channel_multiplier=1))
            pool.sem_inc(mask_ready, 1)
            pool.wait_ge(att_o, run_at["dil"] + 32)
            pool.wait_ge(out_lo, 4)
            done(pool.memset(g_pa[0:32, :], 1.0))
            pool.sem_inc(pa_ones, 1)
            pool.wait_ge(norm_lo, KD * (ORDER["l2"] + 1))
            done(pool.memset(select, 0.0))
            for i in range(2):
                z = select[32 * i:32 * i + 32, :]
                done(pool.affine_select(out=z, in_=z, compare_op=ALU.not_equal, fill=1.0, base=-78,
                                        pattern=[[1, 192]], channel_multiplier=1))
            done(pool.iota(win_dist, pattern=[[1, 3 * P]], base=-P, channel_multiplier=-1,
                           allow_small_or_imprecise_dtypes=True))
            pool.sem_inc(dist_pool, 1)
            pool.wait_ge(dist_abs, 1)
            for sign in (1, -1):
                done(pool.affine_select(out=win_dist, in_=win_dist, compare_op=ALU.is_ge, fill=-NEG, base=P - sign * P,
                                        pattern=[[sign, 3 * P]], channel_multiplier=-sign))
            pool.sem_inc(dist_pool, 1)
            for half in range(2):
                pool.wait_ge(near_made, 8 * (half + 1))
                b = near_bias[half].rearrange("p (q c) -> p q c", c=64)
                for i in range(2):
                    r = slice(64 * i, 64 * i + 64)
                    v = b[r, :, 0:48]
                    done(pool.affine_select(out=v, in_=v, compare_op=ALU.is_ge, fill=NEG, base=8,
                                            pattern=[[0, 56], [1, 48]], channel_multiplier=-1))
                    v = b[r, :, 16:64]
                    done(pool.affine_select(out=v, in_=v, compare_op=ALU.is_ge, fill=NEG, base=7 - 16,
                                            pattern=[[0, 56], [-1, 48]], channel_multiplier=1))
                pool.sem_inc(near_masked, 1)
            pool.wait_ge(norm_lo, KD * (ORDER["l3"] + 1))
            pool.iota(r_dist, pattern=[[1, 7 * P]], base=-3 * P, channel_multiplier=-1,
                      allow_small_or_imprecise_dtypes=True).then_inc(dist_ready, 1)

        @block.scalar
        def _(act):
            chain = Count()

            def split_hi(u, more=0):
                kt = units[u][4] if u < len(units) else KD
                act.wait_ge(raw_in[u % 4], 16 * (u // 4 + 1) + more * 4)
                if u >= 4:
                    act.wait_ge(unit_done, u - 3 + more)
                nc.scalar.copy(whi[:, u % 4, 0:kt, :], raw[:, u % 4, 0:kt, :]).then_inc(hi_done, 1)

            def evacuate(u, more=0):
                act.wait_ge(unit_done, u + 1 + more)
                if u >= 2:
                    act.wait_ge(posted, u - 1 + more)
                kind, which = units[u][0], units[u][5]
                g, s, t = psum[:, u % 2, :], stage[:, u % 2, :], tmp[:, u % 2, :]
                if kind in GATES:
                    if kind == "silu":
                        nc.scalar.copy(s, g)
                        nc.scalar.activation(t, g, ACT.Abs).then_inc(evacuated, 1)
                    else:
                        branch, j = which
                        b = nbias[:, KD * branch + j:KD * branch + j + 1]
                        nc.scalar.activation(s, g, ACT.Relu, scale=-1.0, bias=b)
                        nc.scalar.activation(t, g, ACT.Abs, scale=-1.0, bias=b).then_inc(evacuated, 1)
                elif kind == "head":
                    nc.scalar.copy(s, g)
                    nc.scalar.activation(t, g, ACT.Square).then_inc(evacuated, 1)
                elif kind == "up":
                    nc.scalar.activation(s, g, ACT.Relu).then_inc(evacuated, 1)
                elif kind == "copy" and which[0] in ("k", "gq"):
                    nc.scalar.activation(s, g, ACT.Copy, scale=float(P) ** -0.5).then_inc(evacuated, 1)
                else:
                    nc.scalar.copy(s, g).then_inc(evacuated, 1)

            def continue_with(u):
                kind, t = units[u][0], tmp[:, u % 2, :]
                if kind == "head":
                    act.wait_ge(head_sum, HEADU[u] + 1)
                    nc.scalar.activation(t, XB, ACT.Ln, bias=eps, scale=1.0 / 64).then_inc(act_step, 1)
                    act.wait_ge(act_step, chain.up())
                    nc.scalar.activation(t, t, ACT.Exp, scale=-0.5).then_inc(head_rstd, 1)
                if kind in GATES:
                    act.wait_ge(evacuated, u + 1)
                    nc.scalar.activation(t, t, ACT.Exp, scale=-1.0).then_inc(act_step, 1)
                    act.wait_ge(act_step, chain.up())
                    nc.scalar.activation(t, t, ACT.Ln, bias=1.0).then_inc(gate_ln, 1)

            def gate(u):
                t = tmp[:, u % 2, :]
                act.wait_ge(gate_log, GATEU[u] + 1)
                nc.scalar.activation(t, t, ACT.Exp, scale=1.0 if units[u][0] == "silu" else -1.0).then_inc(gate_exp, 1)

            def decay(h):
                act.wait_ge(ret_exp, h + 1)
                nc.scalar.activation(r_decay[h % 2], r_exp, ACT.Exp).then_inc(ret_decay, 1)

            def ret(h, part):
                if part == 2:
                    act.wait_ge(ret_pv, h + 1)
                    for i in range(2):
                        nc.scalar.copy(r_y[:, i, :], psum[:, 4 + i, :]).then_inc(ret_y, 1)
                if part == 3:
                    act.wait_ge(ret_yc, 2 * h + 2)
                    nc.scalar.activation(r_sq, r_y, ACT.Square).then_inc(ret_sq, 1)
                    if h + 1 < HEADS:
                        decay(h + 1)
                if part == 4:
                    act.wait_ge(ret_var, h + 1)
                    nc.scalar.activation(r_rstd, MB, ACT.Ln, bias=const[:, 1:2], scale=1.0 / (2 * P)).then_inc(act_step, 1)
                    act.wait_ge(act_step, chain.up())
                    nc.scalar.activation(r_rstd, r_rstd, ACT.Exp, scale=-0.5).then_inc(ret_rstd, 1)

            def rates():
                act.wait_ge(norm_lo, KD * (ORDER["l3"] + 1))
                for i, rate in enumerate(("decay_fwd_o_2", "decay_bwd_o_2")):
                    act.dma_start(r_lg[:, 8 * i:8 * i + 8], a[rate].partition_broadcast(P)).then_inc(rate_in, 16)
                act.wait_ge(rate_in, 32)
                nc.scalar.activation(r_lt, r_lg, ACT.Abs).then_inc(act_step, 1)
                act.wait_ge(act_step, chain.up())
                nc.scalar.activation(r_lt, r_lt, ACT.Exp, scale=-1.0).then_inc(act_step, 1)
                act.wait_ge(act_step, chain.up())
                nc.scalar.activation(r_lt, r_lt, ACT.Ln, bias=1.0).then_inc(rate_ready, 1)
                decay(0)

            def att(run, s, k=0):
                if k:
                    return
                at, count = run_at[run], run_n[run]
                i = s - ATT[run][0]
                if 0 <= i < count:
                    g = at + i
                    it = items[g]
                    pt = it["pt"][g % len(it["pt"])]
                    n = len(it["values"])
                    for r in range(-(-n // 4)):
                        act.wait_ge(att_t, rounds[g] + r + 1)
                        if r == 0 and g >= len(it["pt"]):
                            act.wait_ge(att_pv, g - len(it["pt"]) + 1)
                        w = P * min(4, n - 4 * r)
                        nc.scalar.copy(pt[:, 512 * r:512 * r + w], psum[:, 5, 0:w]).then_inc(att_copy, 1)
                if s < count:
                    g = at + s
                    it = items[g]
                    p = it["p"][g % len(it["p"])][:, 0:it["width"]]
                    c = cols[:, g % 4, :]
                    act.wait_ge(att_max, g + 1)
                    if g >= 4:
                        act.wait_ge(att_o, g - 3)
                    if it["sink"] is not None:
                        h = it["sink"]
                        nc.scalar.activation(c[:, 2:3], sinks[:, h:h + 1], ACT.Exp, bias=c[:, 0:1])
                    nc.scalar.activation(p, p, ACT.Exp, bias=c[:, 0:1], accum_out=c[:, 1:2]).then_inc(att_exp, 1)

            def gate_up_load():
                act.dma_start(g_up[0:16, :], a["gla_gate_up"][0]).then_inc(up_in, 16)
                act.dma_start(g_up[16:17, :], a["gla_gate_bias"]).then_inc(up_in, 16)

            def heads_out(half, i):
                n = max(4 * half, 0) + i
                m = out_index(half, i)
                act.wait_ge(out_pe, m + 1)
                nc.scalar.copy(uhi[:, n, :], psum[:, 2 + n % 2, :]).then_inc(out_hi, 1)
                if half < 0 and i == 3:
                    act.wait_ge(out_lo, 3)
                    act.wait_ge(out_pe, 4)
                    gate_up_load()

            def lg(t):
                l = g_e[t % 2]
                act.wait_ge(lg_pe, t + 1)
                if t >= 2:
                    act.wait_ge(lg_done, t - 1)
                nc.scalar.activation(l, psum[:, 2 + t, :], ACT.Abs).then_inc(act_step, 1)
                act.wait_ge(act_step, chain.up())
                nc.scalar.activation(l, l, ACT.Exp, scale=-1.0).then_inc(act_step, 1)
                act.wait_ge(act_step, chain.up())
                nc.scalar.activation(l, l, ACT.Ln, bias=1.0).then_inc(lg_ln, 1)

            def gla(h, part):
                if part == 0:
                    act.wait_ge(gl_b_pe, h + 1)
                    if h:
                        act.wait_ge(gl_out, 2 * h)
                    nc.scalar.copy(g_b, psum[:, 2, :]).then_inc(gl_b, 1)
                if part < 7 or part == 8:
                    n = min(part, 7)
                    act.wait_ge(gl_d, 8 * h + n + 1)
                    e = g_e[part % 2]
                    nc.scalar.activation(e, e, ACT.Abs).then_inc(act_step, 1)
                    act.wait_ge(act_step, chain.up())
                    nc.scalar.activation(e, e, ACT.Exp, scale=-1.0 / 16).then_inc(gl_e, 1)
                if part == 7:
                    act.wait_ge(gl_level, GL * h + 6)
                    nc.scalar.activation(g_e[1], g_b, ACT.Exp, scale=1.0 / 16)
                    nc.scalar.activation(g_last, g_b.rearrange("p (c t) -> p c t", c=NT)[:, :, P - 1], ACT.Exp,
                                         scale=1.0 / 16).then_inc(gl_e, 1)
                if part == 9:
                    act.wait_ge(gl_kt_pe, h + 1)
                    nc.scalar.copy(g_kt, psum[:, 3, :]).then_inc(gl_kt, 1)
                if part == 10:
                    act.wait_ge(gl_pv, h + 1)
                    for i in range(2):
                        nc.scalar.copy(g_head[h % 2][i], psum[:, 4 + i, :]).then_inc(gl_o, 1)
                if part == 11:
                    for i in range(2):
                        act.wait_ge(gl_o, 2 * h + i + 1)
                        nc.scalar.activation(g_qe[i], g_head[h % 2][i], ACT.Square).then_inc(gl_sq, 1)
                    act.wait_ge(gl_sum, h + 1)
                    nc.scalar.activation(g_b, MB, ACT.Ln, bias=eps, scale=1.0 / (2 * P)).then_inc(act_step, 1)
                    act.wait_ge(act_step, chain.up())
                    nc.scalar.activation(g_b, g_b, ACT.Exp, scale=-0.5).then_inc(gl_rstd, 1)

            def bias(half, i):
                if i < 0:
                    act.wait_ge(dist_pool, 1)
                    nc.scalar.activation(win_dist, win_dist, ACT.Abs).then_inc(dist_abs, 1)
                    return
                act.wait_ge(near_sums, 8 * half + i + 1)
                o = near_bias[half].rearrange("p (q c) -> p q c", c=64)[:, :, 8 * i:8 * i + 8]
                nc.scalar.copy(o, psum[:, 2 + i % 2, 0:448].rearrange("p (c q) -> p q c", c=8)).then_inc(near_made, 1)

            def nothing(*_):
                pass

            PARTS = {"ret": ret, "att": att, "heads_out": heads_out, "bias": bias, "lg": lg, "gla": gla, "mask": nothing}

            def static(name):
                if name == "l3":
                    rates()
                if name == "l1":
                    act.wait_ge(vec_ready, 2)
                if name == "l2":
                    act.wait_ge(norm_lo, KD * (ORDER["l2"] + 1))
                    act.dma_start(sinks, a["sink_a_2"].partition_broadcast(P)).then_inc(sink_in, 16)
                    act.dma_start(rpb_rows[0:120, :], a["rpb_b_2"].rearrange("a h j c -> (a h j) c")).then_inc(rpb_in, 16)
                last = first(NORMS[ORDER[name] + 1][0]) - KD
                for u, prev, parts in steps[name]:
                    if prev is not None:
                        evacuate(prev)
                    if u is not None:
                        split_hi(u + 2)
                    soon = any(part[0] == "gla" for part in parts)
                    if soon:
                        for part in parts:
                            gla(*part[1:])
                    if prev is not None:
                        continue_with(prev)
                        squares_after(ORDER[name] + 1, prev - last)
                    for part in parts if not soon else []:
                        PARTS[part[0]](*part[1:])
                    if prev is not None and units[prev][0] in GATES:
                        gate(prev)

            def square(n, k):
                if n:
                    act.wait_ge(posted, first(NORMS[n][0]) - KD + k + 1)
                else:
                    act.wait_ge(x_ready, k + 1)
                if k >= 2:
                    act.wait_ge(norm_sum, (KD - 1) * n + k - 1)
                nc.scalar.activation(tmp[:, k % 2, :], x[:, k, :], ACT.Square).then_inc(norm_sq, 1)

            def squares_after(n, k):
                if n < len(NORMS) and k >= 1:
                    square(n, k - 1)
                    if k == KD - 1:
                        square(n, k)

            def norm(n):
                act.wait_ge(norm_total, n + 1)
                nc.scalar.activation(tmp[:, 0, :], MB, ACT.Ln, bias=eps, scale=1.0 / D).then_inc(act_step, 1)
                act.wait_ge(act_step, chain.up())
                nc.scalar.activation(tmp[:, 1, :], tmp[:, 0, :], ACT.Exp, scale=-0.5).then_inc(norm_rstd, 1)
                for k in range(KD):
                    act.wait_ge(norm_h, KD * n + k + 1)
                    nc.scalar.copy(hhi[:, k, :], hn[:, k, :]).then_inc(norm_hi, 1)

            def ff_block(b, more, following=None):
                for j in range(17):
                    if j:
                        evacuate(b + j - 1, more)
                    if j < 16 and not (following == len(NORMS) and j >= 14):
                        split_hi_ff(b, j + 2, more)
                    if following is not None:
                        squares_after(following, j - 9)

            def split_hi_ff(b, j, more):
                u = b + j
                act.wait_ge(raw_in[u % 4], 16 * (u // 4 + 1) + more * 4)
                act.wait_ge(unit_done, u - 3 + more)
                nc.scalar.copy(whi[:, u % 4, :, :], raw[:, u % 4, :, :]).then_inc(hi_done, 1)

            def ff(i):
                b = steps[f"ff{i}"]
                with act.Fori(0, FB - 1) as f:
                    ff_block(b, f * 16)
                ff_block(b, 16 * (FB - 1), ORDER[f"ff{i}"] + 1)

            act.preload_act_table_set("natural_log_exp_and_others")
            act.wait_ge(const_done, CONSTS)
            for k in range(KD):
                act.wait_ge(x_turned, k + 1)
                nc.scalar.copy(x[:, k, :], psum[:, k % 2, :]).then_inc(x_ready, 1)
                squares_after(0, k)
            split_hi(0)
            split_hi(1)
            for n, (name, _, _) in enumerate(NORMS):
                norm(n)
                if name.startswith("ff"):
                    ff(int(name[2]))
                else:
                    static(name)
            for n in range(2 * NT):
                act.wait_ge(out_turned, n + 1)
                nc.scalar.copy(xout[:, n // 2, 512 * (n % 2):512 * (n % 2) + 512], psum[:, n % 2, :]).then_inc(out_copied, 1)

        @block.vector
        def _(dve):
            chain = Count()

            def split_lo(u, more=0, kt=KD):
                dve.wait_ge(hi_done, u + 1 + more)
                dve.tensor_tensor(wlo[:, u % 4, 0:kt, :], raw[:, u % 4, 0:kt, :], whi[:, u % 4, 0:kt, :].bitcast(F32),
                                  ALU.subtract).then_inc(lo_done, 1)

            def gate_logarithm(u):
                s, t = stage[:, u % 2, :], tmp[:, u % 2, :]
                dve.wait_ge(gate_ln, GATEU[u] + 1)
                if units[u][0] == "silu":
                    dve.scalar_tensor_tensor(out=t, in0=s, scalar=0.0, in1=t, op0=ALU.min,
                                             op1=ALU.subtract).then_inc(gate_log, 1)
                else:
                    dve.tensor_tensor(t, s, t, ALU.add).then_inc(gate_log, 1)

            def post(u, more=0):
                kind, _, _, _, _, j = units[u]
                s = stage[:, u % 2, :]
                dve.wait_ge(evacuated, u + 1 + more)
                if kind == "copy":
                    which, h = j
                    if which == "pa":
                        dve.wait_ge(pa_ones, 1)
                        dve.tensor_copy(g_pa[0:16, :], s[0:16, :]).then_inc(posted, 1)
                    elif which in ("gq", "gk"):
                        dve.tensor_copy(g_head[h % 2][which == "gk"], s).then_inc(posted, 1)
                    else:
                        dve.tensor_copy((r_q if which == "q" else r_k)[h % 2], s).then_inc(posted, 1)
                if kind == "sigmoid":
                    branch, i = j
                    if branch == 0 and i == 0:
                        dve.wait_ge(att_o, run_at["dil"] + 24)
                    dve.wait_ge(gate_exp, GATEU[u] + 1)
                    dve.tensor_copy((mixed if branch == 0 else gate1)[:, i, :], tmp[:, u % 2, :]).then_inc(posted, 1)
                if kind == "branch":
                    branch, i = j
                    if branch == 0:
                        dve.tensor_tensor(mixed[:, i, :], mixed[:, i, :], s, ALU.mult).then_inc(posted, 1)
                    else:
                        t = tmp[:, u % 2, :]
                        dve.tensor_tensor(t, gate1[:, i, :], s, ALU.mult).then_inc(dve_step, 1)
                        dve.wait_ge(dve_step, chain.up())
                        dve.tensor_tensor(t, mixed[:, i, :], t, ALU.add).then_inc(dve_step, 1)
                        dve.wait_ge(dve_step, chain.up())
                        dve.tensor_copy(hhi[:, i, :], t).then_inc(dve_step, 1)
                        dve.wait_ge(dve_step, chain.up())
                        dve.tensor_tensor(hlo[:, i, :], t, hhi[:, i, :].bitcast(F32), ALU.subtract).then_inc(posted, 1)
                if kind == "turn":
                    if j[0] == "a":
                        o = e_v
                    elif j[0] == "b":
                        o = n_v[j[1] % 2]
                        if j[1] >= 2:
                            dve.wait_ge(att_o, run_at["near"] + 8 * (j[1] - 1))
                    elif j[0] == "d":
                        o = d_v[j[1] % 2][:, :, P * j[2]:P * j[2] + P]
                    elif j[0] == "g":
                        o = g_head[j[1] % 2][2][:, :, P * j[2]:P * j[2] + P]
                    else:
                        o = r_v[j[0] % 2][:, :, P * j[1]:P * j[1] + P]
                    dve.wait_ge(turned, TURNS[u] + 1)
                    dve.tensor_copy(o, XB.rearrange("p (t c) -> p t c", t=NT)).then_inc(posted, 1)
                if kind == "head":
                    layer, which, i = j[:3]
                    t = tmp[:, u % 2, :]
                    g = VROWS + {"d": 0, "a": 2, "b": 4}[layer] + (which == "k")
                    if layer == "d":
                        o = (d_q if which == "q" else d_k)[i % 2][:, j[3], :]
                        if i >= 2:
                            dve.wait_ge(att_o, run_at["dil"] + 8 * (i - 1))
                    if layer == "a":
                        o = e_q[:, i, :] if which == "q" else e_k
                    if layer == "b":
                        o = (n_q if which == "q" else n_k)[i % 2]
                        if i >= 2:
                            dve.wait_ge(att_o, run_at["near"] + 8 * (i - 1))
                    dve.wait_ge(head_rstd, HEADU[u] + 1)
                    ins = dve.scalar_tensor_tensor(out=o, in0=s, scalar=vec[:, g:g + 1], in1=t, op0=ALU.mult, op1=ALU.mult)
                    if layer == "a" and which == "k":
                        ins.then_inc(dve_step, 1)
                        dve.wait_ge(dve_step, chain.up())
                        dve.tensor_copy(e_k2[0:64, :], e_k[64:128, :]).then_inc(dve_step, 1)
                        dve.wait_ge(dve_step, chain.up())
                        ins = dve.tensor_copy(e_k2[64:128, :], e_k[0:64, :])
                    ins.then_inc(posted, 1)
                if kind == "silu":
                    h, i = j[-2:]
                    dest = g_head[h % 2][3] if j[0] == "g" else r_g[h % 2]
                    dve.wait_ge(gate_exp, GATEU[u] + 1)
                    dve.tensor_tensor(dest[:, i, :], s, tmp[:, u % 2, :], ALU.mult).then_inc(posted, 1)
                if kind in ("down", "mix"):
                    dve.tensor_tensor(x[:, j, :], x[:, j, :], s, ALU.add).then_inc(posted, 1)
                if kind == "up":
                    t = tmp[:, u % 2, :]
                    dve.tensor_tensor(t, s, s, ALU.mult).then_inc(dve_step, 1)
                    dve.wait_ge(dve_step, chain.up())
                    dve.tensor_copy(uhi[:, j, :], t).then_inc(dve_step, 1)
                    dve.wait_ge(dve_step, chain.up())
                    dve.tensor_tensor(ulo[:, j, :], t, uhi[:, j, :].bitcast(F32), ALU.subtract).then_inc(posted, 1)

            def decay(h):
                dve.wait_ge(ret_decay, h) if h else dve.wait_ge(dist_ready, 1)
                dve.tensor_scalar(r_exp, r_dist, r_lt[:, 8 + h:9 + h], None, ALU.mult).then_inc(dve_step, 1)
                dve.wait_ge(dve_step, chain.up())
                dve.scalar_tensor_tensor(out=r_exp, in0=r_dist, scalar=r_lg[:, h:h + 1], in1=r_exp,
                                         op0=ALU.mult, op1=ALU.min).then_inc(ret_exp, 1)

            def rates():
                dve.wait_ge(rate_ready, 1)
                dve.scalar_tensor_tensor(out=r_lg, in0=r_lg, scalar=0.0, in1=r_lt, op0=ALU.min,
                                         op1=ALU.subtract).then_inc(dve_step, 1)
                dve.wait_ge(dve_step, chain.up())
                dve.tensor_scalar(r_lt, r_lg, -1.0, None, ALU.mult).then_inc(dve_step, 1)
                dve.wait_ge(dve_step, chain.up())
                decay(0)

            def ret(h, part):
                if part < 2:
                    for j in (2 * part, 2 * part + 1):
                        dve.wait_ge(ret_qk, NT * h + j + 1)
                        if j == 0:
                            dve.wait_ge(ret_decay, h + 1)
                        dve.tensor_tensor(r_a[:, j, :], psum[:, 2 + j % 2, :],
                                          r_decay[h % 2][:, (3 - j) * P:(3 - j) * P + SEQ], ALU.mult).then_inc(ret_a, 1)
                if part == 3:
                    dve.wait_ge(ret_mean, h + 1)
                    for i in range(2):
                        dve.scalar_tensor_tensor(out=r_y[:, i, :], in0=MB, scalar=-1.0 / (2 * P), in1=r_y[:, i, :],
                                                 op0=ALU.mult, op1=ALU.add).then_inc(ret_yc, 1)
                if part == 4:
                    dve.wait_ge(ret_rstd, h + 1)
                    dve.wait_ge(posted, UNIT_OF["silu", "w_in_o_2", 0, 4 * D + 2 * P * h + P] + 1)
                    if h == 4:
                        dve.wait_ge(unit_done, UNIT_OF["down", "w_out_o_2", 0, D - P] + 1)
                    for i in range(2):
                        y = r_y[:, i, :]
                        j = 2 * (h % 4) + i
                        dve.scalar_tensor_tensor(out=y, in0=y, scalar=gain("ret_gn_o_2", 2 * h + i), in1=r_rstd,
                                                 op0=ALU.mult, op1=ALU.mult).then_inc(dve_step, 1)
                        dve.wait_ge(dve_step, chain.up())
                        dve.tensor_tensor(y, y, r_g[h % 2][:, i, :], ALU.mult).then_inc(dve_step, 1)
                        dve.wait_ge(dve_step, chain.up())
                        dve.tensor_copy(uhi[:, j, :], y).then_inc(dve_step, 1)
                        dve.wait_ge(dve_step, chain.up())
                        dve.tensor_tensor(ulo[:, j, :], y, uhi[:, j, :].bitcast(F32), ALU.subtract).then_inc(ret_out, 1)
                if part == 2 and h + 1 < HEADS:
                    decay(h + 1)

            def att(run, s, k=0):
                if k:
                    return
                at, count = run_at[run], run_n[run]
                i = s - ATT[run][1]

                def softmax():
                    g = at + s
                    it = items[g]
                    p = it["p"][g % len(it["p"])]
                    c = cols[:, g % 4, :]
                    if run == "win" and s % NT == 0:
                        h = it["h"]
                        if h == 0:
                            dve.wait_ge(dist_pool, 2)
                        dve.tensor_scalar(win_bias[h % 2], win_dist, -2.0 ** -(h + 1), None, ALU.mult).then_inc(dve_step, 1)
                        dve.wait_ge(dve_step, chain.up())
                    if run == "dil" and s == 0:
                        dve.wait_ge(mask_ready, 1)
                    if run == "near" and s % 16 == 0:
                        dve.wait_ge(near_masked, s // 16 + 1)
                    dve.wait_ge(att_qk, g + 1)
                    if g >= len(it["p"]):
                        dve.wait_ge(att_t, rounds[g - len(it["p"]) + 1])
                    for c0, b, q, k, bias in it["segments"]:
                        w = k.shape[1]
                        ins = dve.scalar_tensor_tensor(out=p[:, c0:c0 + w], in0=psum[:, 2 + b, 0:w], scalar=it["scale"],
                                                       in1=bias, op0=ALU.mult, op1=ALU.add)
                    ins.then_inc(att_sm, 1)
                    dve.wait_ge(att_sm, g + 1)
                    if g >= 4:
                        dve.wait_ge(att_o, g - 3)
                    if it["sink"] is None:
                        dve.tensor_reduce(c[:, 0:1], p[:, 0:it["width"]], AX.X, ALU.max, negate=True).then_inc(att_max, 1)
                    else:
                        dve.tensor_reduce(c[:, 0:1], p[:, 0:it["width"]], AX.X, ALU.max, negate=True).then_inc(dve_step, 1)
                        dve.wait_ge(dve_step, chain.up())
                        h = it["sink"]
                        dve.tensor_tensor(c[:, 0:1], c[:, 0:1], sinks_neg[:, h:h + 1], ALU.min).then_inc(att_max, 1)

                def normalise():
                    g = at + i
                    it = items[g]
                    c = cols[:, g % 4, :]
                    dve.wait_ge(att_exp, g + 1)
                    den = c[:, 1:2]
                    if it["sink"] is not None:
                        dve.tensor_tensor(c[:, 2:3], den, c[:, 2:3], ALU.add).then_inc(dve_step, 1)
                        dve.wait_ge(dve_step, chain.up())
                        den = c[:, 2:3]
                    dve.reciprocal(c[:, 3:4], den).then_inc(dve_step, 1)
                    dve.wait_ge(dve_step, chain.up())
                    dve.wait_ge(att_pv, g + 1)
                    dve.tensor_scalar(it["out"], MB[:, 0:E], c[:, 3:4], None, ALU.mult).then_inc(att_o, 1)

                if run == "dil" and 0 <= i < count:
                    normalise()
                if s < count:
                    softmax()
                if run != "dil" and 0 <= i < count:
                    normalise()

            def heads_out(half, i):
                n = max(4 * half, 0) + i
                dve.wait_ge(out_hi, out_index(half, i) + 1)
                dve.tensor_tensor(ulo[:, n, :], psum[:, 2 + n % 2, :], uhi[:, n, :].bitcast(F32), ALU.subtract).then_inc(out_lo, 1)

            def mask():
                dve.wait_ge(mask_sums, 1)
                dve.memset(d_bias[:, 0:256], 0.0)
                for i in range(2):
                    for c in range(NT):
                        o = 256 + 512 * i + P * c
                        ins = dve.tensor_scalar(d_bias[:, o:o + P], psum[:, 2, P * i:P * i + P], -NEG, NEG, ALU.mult, ALU.add)
                ins.then_inc(mask_copied, 1)

            def lg(t):
                dve.wait_ge(lg_ln, t + 1)
                dve.scalar_tensor_tensor(out=g_lg[:, t, :], in0=psum[:, 2 + t, :], scalar=0.0, in1=g_e[t % 2],
                                         op0=ALU.min, op1=ALU.subtract).then_inc(lg_done, 1)

            def gla(h, part):
                q, k, v, r = g_head[h % 2]
                k_n = 9 * h
                b3 = g_b.rearrange("p (c t) -> p c t", c=NT)

                def difference(n):
                    m = HALVINGS[n] if n < 7 else P // 2
                    at_ = m - 1 if n < 7 else P - 1
                    blocks = g_b.rearrange("p (b t) -> p b t", t=2 * m)
                    e = g_e[n % 2].rearrange("p (b t) -> p b t", t=2 * m)
                    if n >= 2:
                        dve.wait_ge(gl_level, GL * h + n - 1)
                    elif h:
                        dve.wait_ge(gl_kt_pe, h)
                    ref = blocks[:, :, at_:at_ + 1].to_broadcast([P, SEQ // (2 * m), 2 * m])
                    dve.tensor_tensor(e, blocks, ref, ALU.subtract).then_inc(gl_d, 1)

                def factors(n):
                    dve.wait_ge(gl_e, k_n + n + 1)
                    e = g_e[n % 2]
                    dve.tensor_tensor(g_qe[n % 2], q, e, ALU.mult)
                    dve.tensor_tensor(e, k, e, ALU.mult).then_inc(gl_f, 1)

                if part == 0:
                    dve.wait_ge(gl_b, h + 1)
                    difference(0)
                if 1 <= part <= 7:
                    factors(part - 1)
                    if part < 7:
                        difference(part)
                if part == 5:
                    dve.wait_ge(gl_level, GL * h + 2)
                    if h:
                        dve.wait_ge(gl_pv, h)
                    else:
                        dve.memset(g_a, 0.0).then_inc(dve_step, 1)
                        dve.wait_ge(dve_step, chain.up())
                    dve.tensor_copy(g_a[0:64, :, 64:128], psum[0:64, 3, 0:256].rearrange("p (c t) -> p c t", c=NT))
                    for j in range(2):
                        ins = dve.tensor_copy(g_a[64 * j:64 * j + 32, :, 64 * j + 32:64 * j + 64],
                                              psum[64 * j:64 * j + 32, 3, 256:384].rearrange("p (c t) -> p c t", c=NT))
                    ins.then_inc(gl_a, 1)
                if part == 8:
                    dve.wait_ge(gl_level, GL * h + 6)
                    dve.wait_ge(gl_e, k_n + 8)
                    dve.tensor_tensor(g_qe[1], q, g_e[1], ALU.mult).then_inc(gl_f, 1)
                    difference(8)
                    dve.wait_ge(gl_e, k_n + 9)
                    dve.tensor_tensor(g_e[0], k, g_e[0], ALU.mult).then_inc(gl_f, 1)
                if part == 9:
                    dve.wait_ge(gl_level, GL * h + 8)
                    for i in range(6):
                        src = psum[:, 4 + i // 4, P * (i % 4):P * (i % 4) + P].rearrange("p (c t) -> p c t", c=NT)
                        m = g_mask[:, i:i + 1, :].to_broadcast([P, NT, 32])
                        ins = dve.tensor_tensor(g_small[:, i, :].rearrange("p (c t) -> p c t", c=NT), src, m, ALU.mult)
                    ins.then_inc(dve_step, 1)
                    dve.wait_ge(dve_step, chain.up())
                    for step in (3, 1, 1):
                        if step == 3:
                            dve.tensor_tensor(g_small[:, 0:3, :], g_small[:, 0:3, :], g_small[:, 3:6, :], ALU.add)\
                               .then_inc(dve_step, 1)
                            src = 1
                        else:
                            dve.tensor_tensor(g_small[:, 0, :], g_small[:, 0, :], g_small[:, src, :], ALU.add)\
                               .then_inc(dve_step, 1)
                            src += 1
                        dve.wait_ge(dve_step, chain.up())
                    for j in range(4):
                        s_ = slice(32 * j, 32 * j + 32)
                        ins = dve.tensor_copy(g_a[s_, :, s_], g_small[s_, 0, :].rearrange("p (c t) -> p c t", c=NT))
                    ins.then_inc(gl_a, 1)
                if part == 10:
                    for c in range(NT - 1):
                        dve.wait_ge(gl_upd, 3 * h + c + 1)
                        new, old = g_states[(c + 1) % 2], g_states[c % 2]
                        if c == 0:
                            dve.tensor_copy(new, psum[:, 2, 0:256]).then_inc(gl_state, 1)
                        else:
                            dve.wait_ge(gl_state, 3 * h + c)
                            dve.scalar_tensor_tensor(out=new, in0=old, scalar=g_last[:, c:c + 1],
                                                     in1=psum[:, 2, 0:256], op0=ALU.mult, op1=ALU.add).then_inc(gl_state, 1)
                if part == 11:
                    dve.wait_ge(gl_rstd, h + 1)
                    dve.wait_ge(posted, UNIT_OF["silu", "w_in", 0, RG + 2 * P * h + P] + 1)
                    for i in range(2):
                        y = g_head[h % 2][i]
                        j = 2 * h + i
                        dve.scalar_tensor_tensor(out=y, in0=y, scalar=gain("gla_out_norm_g", i), in1=g_b,
                                                 op0=ALU.mult, op1=ALU.mult).then_inc(dve_step, 1)
                        dve.wait_ge(dve_step, chain.up())
                        dve.tensor_tensor(y, y, r[:, i, :], ALU.mult).then_inc(dve_step, 1)
                        dve.wait_ge(dve_step, chain.up())
                        dve.tensor_copy(uhi[:, j, :], y).then_inc(dve_step, 1)
                        dve.wait_ge(dve_step, chain.up())
                        dve.tensor_tensor(ulo[:, j, :], y, uhi[:, j, :].bitcast(F32), ALU.subtract).then_inc(gl_out, 1)

            def bias(half, i):
                if i < 0:
                    dve.wait_ge(sink_in, 16)
                    dve.tensor_scalar(sinks_neg, sinks, -1.0, None, ALU.mult).then_inc(dve_step, 1)
                    dve.wait_ge(dve_step, chain.up())
                    dve.wait_ge(rpb_turned, 1)
                    for half in range(2):
                        src = psum[0:31, 5, 0:120].rearrange("p (h j) -> p h j", h=8)[:, :, 1 - half:15 - half]
                        dve.tensor_copy(rpb_cols[32 * half:32 * half + 31, :].rearrange("p (h j) -> p h j", h=8), src)\
                           .then_inc(rpb_ready, 1)

            PARTS = {"ret": ret, "att": att, "heads_out": heads_out, "bias": bias, "lg": lg, "gla": gla, "mask": mask}

            def static(name):
                if name == "l3":
                    rates()
                last = first(NORMS[ORDER[name] + 1][0]) - KD
                for u, prev, parts in steps[name]:
                    soon = any(part[0] == "gla" for part in parts)
                    if soon:
                        for part in parts:
                            gla(*part[1:])
                    if u is not None:
                        split_lo(u + 2, kt=units[u + 2][4])
                    late = prev is not None and units[prev][0] in GATES
                    if late:
                        gate_logarithm(prev)
                    elif prev is not None:
                        post(prev)
                        squares_after(ORDER[name] + 1, prev - last)
                    for part in parts if not soon else []:
                        PARTS[part[0]](*part[1:])
                    if late:
                        post(prev)

            def add_squares(n, k):
                dve.wait_ge(norm_sq, KD * n + k + 1)
                if k == 0:
                    dve.tensor_copy(squares[:, :], tmp[:, 0, :]).then_inc(norm_sum, 1)
                else:
                    dve.wait_ge(norm_sum, (KD - 1) * n + k)
                    dve.tensor_tensor(squares[:, :], squares[:, :], tmp[:, k % 2, :], ALU.add).then_inc(norm_sum, 1)

            def squares_after(n, k):
                if n < len(NORMS) and k >= 1:
                    add_squares(n, k - 1)

            def norm(n):
                _, name, k0 = NORMS[n]
                dve.wait_ge(norm_rstd, n + 1)
                for k in range(KD + 1):
                    if k < KD:
                        dve.scalar_tensor_tensor(out=hn[:, k, :], in0=x[:, k, :], scalar=gain(name, k0 + k),
                                                 in1=tmp[:, 1, :], op0=ALU.mult, op1=ALU.mult).then_inc(norm_h, 1)
                    if k:
                        dve.wait_ge(norm_hi, KD * n + k)
                        dve.tensor_tensor(hlo[:, k - 1, :], hn[:, k - 1, :], hhi[:, k - 1, :].bitcast(F32),
                                          ALU.subtract).then_inc(norm_lo, 1)

            def ff_block(b, more, following=None):
                for j in range(17):
                    if j < 16 and not (following == len(NORMS) and j >= 14):
                        split_lo(b + j + 2, more)
                    if j:
                        post(b + j - 1, more)
                        if following is not None:
                            squares_after(following, j - 9)

            def ff(i):
                b = steps[f"ff{i}"]
                with dve.Fori(0, FB - 1) as f:
                    chain.loop = f * 16
                    n0 = chain.n
                    ff_block(b, f * 16)
                    assert chain.n == n0 + 16
                chain.n += 16 * (FB - 2)
                chain.loop = 0
                ff_block(b, 16 * (FB - 1), ORDER[f"ff{i}"] + 1)

            dve.wait_ge(const_done, CONSTS)
            for k in range(KD - 1):
                add_squares(0, k)
            dve.wait_ge(x_turned, KD + 1)
            dve.tensor_copy(vec[:, 0:VALL], MB[:, 0:VALL]).then_inc(vec_ready, 1)
            dve.wait_ge(vec_ready, 1)
            b0 = VEC["branch_gate_bias"][0]
            split_lo(0)
            split_lo(1)
            dve.tensor_scalar(nbias[:, :], vec[:, b0:b0 + 16], -1.0, None, ALU.mult).then_inc(vec_ready, 1)
            for n, (name, _, _) in enumerate(NORMS):
                norm(n)
                if name.startswith("ff"):
                    ff(int(name[2]))
                else:
                    static(name)

        @block.tensor
        def _(pe):
            mix0, gla_branch0 = UNIT_OF["mix", "w_out", 0, 0], UNIT_OF["branch", "w_gla_branch", 0, 0]
            norm_before = {first(n[0]): i for i, n in enumerate(NORMS)}

            def products(u, n0, n1, hi, lo, more=0):
                kt = units[u][4]
                g = psum[:, u % 2, :]
                for n in range(n0, n1):
                    k, part = divmod(n, 3)
                    if u in norm_before and part == 0:
                        pe.wait_ge(norm_lo, KD * norm_before[u] + k + 1)
                    if u == mix0 and part == 0:
                        pe.wait_ge(posted, gla_branch0 + k + 1)
                    w, v = ((whi, hi), (whi, lo), (wlo, hi))[part]
                    mm = pe.matmul(g, w[:, u % 4, k, :], v[:, k, :], start=n == 0, stop=n == 3 * kt - 1)
                if n1 == 3 * kt:
                    mm.then_inc(unit_done, 1)

            def begin(u, more=0):
                pe.wait_ge(lo_done, u + 1 + more)
                if u >= 2:
                    pe.wait_ge(evacuated, u - 1 + more)

            def shared_bank(u):
                if u not in shared_before:
                    return
                pe.wait_ge(evacuated, u + 1)
                if shared_before[u] is not None:
                    pe.wait_ge(posted, shared_before[u] + 1)
                if units[u][0] == "turn":
                    for t in range(NT):
                        mm = pe.transpose(XB[:, P * t:P * t + P], stage[:, u % 2, P * t:P * t + P], ident[:, :])
                    mm.then_inc(turned, 1)
                else:
                    pe.matmul(XB, bones[:, :], tmp[:, u % 2, :], start=True, stop=True).then_inc(head_sum, 1)

            def ret(h, part):
                q, k, v = r_q[h % 2], r_k[h % 2], r_v[h % 2]
                if part < 2:
                    for j in (2 * part, 2 * part + 1):
                        if j == 0:
                            pe.wait_ge(posted, UNIT_OF["turn", "w_in_o_2", 0, 2 * D + 2 * P * h + P] + 1)
                        if NT * h + j >= 2:
                            pe.wait_ge(ret_a, NT * h + j - 1)
                        pe.matmul(psum[:, 2 + j % 2, :], k[:, P * j:P * j + P], q, start=True, stop=True).then_inc(ret_qk, 1)
                if part == 2:
                    if h:
                        pe.wait_ge(ret_y, 2 * h)
                    for j in range(NT):
                        pe.wait_ge(ret_a, NT * h + j + 1)
                        for i in range(2):
                            mm = pe.matmul(psum[:, 4 + i, :], v[:, j, P * i:P * i + P], r_a[:, j, :],
                                           start=j == 0, stop=j == NT - 1)
                    mm.then_inc(ret_pv, 1)
                if part in (3, 4):
                    if part == 3:
                        pe.wait_ge(ret_y, 2 * h + 2)
                        if h:
                            pe.wait_ge(ret_rstd, h)
                    else:
                        pe.wait_ge(ret_sq, h + 1)
                    src = r_y if part == 3 else r_sq
                    for i in range(2):
                        mm = pe.matmul(MB, ones[:, :], src[:, i, :], start=i == 0, stop=i == 1)
                    mm.then_inc(ret_mean if part == 3 else ret_var, 1)

            def att(run, s, k=0):
                at, count = run_at[run], run_n[run]
                turn_lag, use_lag = ATT[run]

                def scores():
                    g = at + s
                    it = items[g]
                    pe.wait_ge(posted, it["unit"] + 1)
                    back = 3 if run != "dil" else 1
                    if s == 0:
                        if g:
                            pe.wait_ge(att_o, g)
                        if run == "dil":
                            pe.wait_ge(mask_copied, 1)
                        else:
                            pe.wait_ge(near_made, {"win": 8, "near": 16}[run])
                    elif s >= back:
                        pe.wait_ge(att_sm, g - back + 1)
                    for _, b, q, k, _ in it["segments"]:
                        mm = pe.matmul(psum[:, 2 + b, 0:k.shape[1]], q, k, start=True, stop=True)
                    mm.then_inc(att_qk, 1)

                def use(g):
                    it = items[g]
                    pt = it["pt"][g % len(it["pt"])]
                    pe.wait_ge(att_copy, rounds[g + 1])
                    if g:
                        pe.wait_ge(att_o, g)
                    n = len(it["values"])
                    for b in range(n):
                        mm = pe.matmul(MB[:, 0:E], pt[:, P * b:P * b + P], it["values"][b], start=b == 0, stop=b == n - 1)
                    mm.then_inc(att_pv, 1)

                def turn(g, only=None):
                    it = items[g]
                    p = it["p"][g % len(it["p"])]
                    pe.wait_ge(att_exp, g + 1)
                    n = len(it["values"])
                    for r in range(-(-n // 4)):
                        if only is not None and r != only:
                            continue
                        if rounds[g] + r:
                            pe.wait_ge(att_copy, rounds[g] + r)
                        for b in range(4 * r, min(4 * r + 4, n)):
                            mm = pe.transpose(psum[:, 5, P * (b % 4):P * (b % 4) + P], p[:, P * b:P * b + P], ident[:, :])
                        mm.then_inc(att_t, 1)

                if run == "dil":
                    if k == 0 and 0 <= s - use_lag < count:
                        use(at + s - use_lag)
                    if k == 0 and s < count:
                        scores()
                    if k and 0 <= s - turn_lag < count:
                        turn(at + s - turn_lag, k - 1)
                    return
                if s < count:
                    scores()
                if 0 <= s - use_lag < count:
                    use(at + s - use_lag)
                if 0 <= s - turn_lag < count:
                    turn(at + s - turn_lag)

            def heads_out(half, i):
                n = max(4 * half, 0) + i
                m = out_index(half, i)
                first_layer = half < 0
                if i == 0:
                    if first_layer:
                        pe.wait_ge(att_o, 32)
                    else:
                        pe.wait_ge(att_o, run_at["near"] + (32 if half else 0))
                if i >= 2 or half == 1:
                    pe.wait_ge(out_lo, m - 1)
                src = d_heads if first_layer else heads
                for t in range(NT):
                    mm = pe.transpose(psum[:, 2 + n % 2, P * t:P * t + P], src[:, t, P * i:P * i + P], ident[:, :])
                mm.then_inc(out_pe, 1)

            def mask():
                pe.wait_ge(pick_ready, 1)
                for i, m in enumerate((4, 16)):
                    mm = pe.matmul(psum[:, 2, P * i:P * i + P], d_pick[0:m, i, :], d_pick[0:m, i, :], start=True, stop=True)
                mm.then_inc(mask_sums, 1)

            def lg(t):
                if t == 0:
                    pe.wait_ge(up_in, 32)
                    pe.wait_ge(posted, UNIT_OF["copy", "w_in", 0, PA] + 1)
                    pe.wait_ge(out_lo, 4)
                pe.matmul(psum[:, 2 + t, :], g_pa[0:17, P * t:P * t + P], g_up[0:17, :], start=True, stop=True).then_inc(lg_pe, 1)

            def gla(h, part):
                q, k, v, r = g_head[h % 2]

                def level(n):
                    if n < 7:
                        pe.wait_ge(gl_f, 9 * h + n + 1)
                        ke, qe = g_e[n % 2], g_qe[n % 2]
                    else:
                        ke, qe = k, q
                    if n == 0:
                        for c in range(NT):
                            mm = pe.matmul(psum[0:64, 3, 64 * c:64 * c + 64], ke[:, P * c:P * c + 64],
                                           qe[:, P * c + 64:P * c + P], start=True, stop=True)
                    elif n == 1:
                        for c in range(NT):
                            for j in range(2):
                                o = P * c + 64 * j
                                mm = pe.matmul(psum[64 * j:64 * j + 32, 3, 256 + 32 * c:288 + 32 * c], ke[:, o:o + 32],
                                               qe[:, o + 32:o + 64], start=True, stop=True)
                    else:
                        i = n - 2
                        for c in range(NT):
                            for j in range(4):
                                o = P * c + 32 * j
                                at_ = P * (i % 4) + 32 * c
                                mm = pe.matmul(psum[32 * j:32 * j + 32, 4 + i // 4, at_:at_ + 32], ke[:, o:o + 32],
                                               qe[:, o:o + 32], start=True, stop=True)
                    mm.then_inc(gl_level, 1)

                if part == 0:
                    pe.wait_ge(posted, UNIT_OF["turn", "w_in", 0, VG + 2 * P * h + P] + 1)
                    if h == 0:
                        pe.wait_ge(lg_done, NT)
                    else:
                        pe.wait_ge(gl_state, 3 * h)
                    for c in range(NT):
                        mm = pe.matmul(psum[:, 2, P * c:P * c + P], g_lg[:, c, P * h:P * h + P], tri[:, :], start=True, stop=True)
                    mm.then_inc(gl_b_pe, 1)
                if part == 2:
                    if h:
                        pe.wait_ge(gl_kt, h)
                        pe.wait_ge(gl_o, 2 * h)
                if 2 <= part <= 8:
                    level(part - 2)
                if part == 8:
                    level(7)
                if part == 9:
                    pe.wait_ge(gl_f, 9 * h + 9)
                    pe.wait_ge(gl_a, 2 * h + 1)
                    for c in range(NT):
                        mm = pe.transpose(psum[:, 3, P * c:P * c + P], g_e[0][:, P * c:P * c + P], ident[:, :])
                    mm.then_inc(gl_kt_pe, 1)
                if part == 10:
                    pe.wait_ge(gl_a, 2 * h + 2)
                    pe.wait_ge(gl_kt, h + 1)
                    for c in range(NT):
                        if c:
                            pe.wait_ge(gl_state, 3 * h + c)
                        if c < NT - 1:
                            pe.matmul(psum[:, 2, 0:256], g_kt[:, c, :], v[:, c, :], start=True, stop=True).then_inc(gl_upd, 1)
                        for i in range(2):
                            o = psum[:, 4 + i, P * c:P * c + P]
                            mm = pe.matmul(o, v[:, c, P * i:P * i + P], g_a[:, c, :], start=True, stop=c == 0)
                            if c:
                                mm = pe.matmul(o, g_states[c % 2][:, P * i:P * i + P], g_qe[1][:, P * c:P * c + P],
                                               start=False, stop=True)
                    mm.then_inc(gl_pv, 1)
                if part == 11:
                    for i in range(2):
                        pe.wait_ge(gl_sq, 2 * h + i + 1)
                        mm = pe.matmul(MB, ones[:, :], g_qe[i], start=i == 0, stop=i == 1)
                    mm.then_inc(gl_sum, 1)

            def bias(half, i):
                if i < 0:
                    pe.wait_ge(rpb_in, 16)
                    pe.transpose(psum[0:31, 5, 0:120], rpb_rows[0:120, :], ident[0:120, 0:120]).then_inc(rpb_turned, 1)
                    return
                if i == 0:
                    pe.wait_ge(rpb_ready, 2)
                    pe.wait_ge(dist_pool, 1)
                    if half:
                        pe.wait_ge(out_lo, OUT0 + 4)
                if i >= 2:
                    pe.wait_ge(near_made, 8 * half + i - 1)
                for c in range(8):
                    z = 63 - (8 * i + c)
                    for low in range(2):
                        r = slice(32 * low, 32 * low + 31)
                        mm = pe.matmul(psum[64 * low:64 * low + 64, 2 + i % 2, 56 * c:56 * c + 56], select[r, z:z + 64],
                                       rpb_cols[r, 56 * half:56 * half + 56], start=True, stop=True)
                mm.then_inc(near_sums, 1)

            PARTS = {"ret": ret, "att": att, "heads_out": heads_out, "bias": bias, "lg": lg, "gla": gla, "mask": mask,
                     "shared_bank": shared_bank}
            def operands_ready(u):
                names = units[u][:4]
                if names == ("branch", "w_attn_branch", 0, 0):
                    pe.wait_ge(out_lo, 4)
                if names == ("branch", "w_gla_branch", 0, 0):
                    pe.wait_ge(gl_out, 8)
                if names == ("down", "w_out_e_2", 0, 0):
                    pe.wait_ge(out_lo, OUT0 + 4)
                if names == ("down", "w_out_e_2", 512, 0):
                    pe.wait_ge(out_lo, OUT0 + 8)
                if names == ("down", "w_out_o_2", 0, 0):
                    pe.wait_ge(ret_out, 8)
                if names == ("down", "w_out_o_2", D, 0):
                    pe.wait_ge(ret_out, 12)
                if names == ("down", "w_out_o_2", D + 4 * P, 0):
                    pe.wait_ge(ret_out, 16)

            def static(name):
                for u, prev, parts in steps[name]:
                    if u is not None:
                        begin(u)
                        total = 3 * units[u][4]
                        k0 = units[u][2] % D // P
                        operand = (uhi[:, k0:, :], ulo[:, k0:, :]) if units[u][0] in ("down", "branch") else (hhi, hlo)
                        operands_ready(u)
                    soon = any(part[0] == "gla" for part in parts)
                    between = [("shared_bank", prev)] * (prev is not None)
                    between = parts + between if soon else between + parts
                    n = len(between) + 1
                    for i, part in enumerate(between):
                        if u is not None:
                            products(u, total * i // n, total * (i + 1) // n, *operand)
                        PARTS[part[0]](*part[1:])
                    if u is not None:
                        products(u, total * (n - 1) // n, total, *operand)

            def norm(n):
                pe.wait_ge(norm_sum, (KD - 1) * (n + 1))
                pe.matmul(MB, ones[:, :], squares[:, :], start=True, stop=False)
                pe.wait_ge(norm_sq, KD * (n + 1))
                pe.matmul(MB, ones[:, :], tmp[:, (KD - 1) % 2, :], start=False, stop=True).then_inc(norm_total, 1)

            def ff(i):
                b = steps[f"ff{i}"]
                with pe.Fori(0, FB) as f:
                    for j in range(16):
                        u = b + j
                        begin(u, f * 16)
                        for k in range(KD):
                            if j == 8:
                                pe.wait_ge(posted, b + k + 1 + f * 16)
                            products(u, 3 * k, 3 * k + 3, *((hhi, hlo) if j < 8 else (uhi, ulo)))

            pe.wait_ge(const_done, CONSTS)
            for k in range(KD):
                if k % 4 == 0:
                    pe.wait_ge(x_in[k // 4], 16)
                if k >= 2:
                    pe.wait_ge(x_ready, k - 1)
                for t in range(NT):
                    mm = pe.transpose(psum[:, k % 2, P * t:P * t + P], xin[:, t, P * k:P * k + P], ident[:, :])
                mm.then_inc(x_turned, 1)
            pe.wait_ge(vec_in, 16 * (len(VEC) + 2 * len(HEADVEC)))
            pe.transpose(MB[:, 0:VALL], rows[0:VALL, :], ident[0:VALL, 0:VALL]).then_inc(x_turned, 1)
            pe.wait_ge(x_ready, KD)
            pe.wait_ge(vec_ready, 1)
            for n, (name, _, _) in enumerate(NORMS):
                norm(n)
                if name.startswith("ff"):
                    ff(int(name[2]))
                else:
                    static(name)
            pe.wait_ge(posted, len(units))
            for n in range(2 * NT):
                if n >= 2:
                    pe.wait_ge(out_copied, n - 1)
                for k in range(4):
                    mm = pe.transpose(psum[:, n % 2, P * k:P * k + P],
                                      x[:, 4 * (n % 2) + k, P * (n // 2):P * (n // 2) + P], ident[:, :])
                mm.then_inc(out_turned, 1)


def kernel(**inputs):
    import numpy as _np
    import concourse.bacc as _bacc
    from concourse.bass_utils import run_bass_kernel_spmd as _run

    nc = _bacc.Bacc("TRN2", target_bir_lowering=False, num_devices=1)
    arrays, args = {}, {}
    for name, value in inputs.items():
        v = _np.ascontiguousarray(value)
        arrays[f"in_{name}_dram"] = v
        args[name] = nc.dram_tensor(f"in_{name}_dram", v.shape, mybir.dt.from_np(v.dtype), kind="ExternalInput").ap()
    out = nc.dram_tensor("out_0_dram", (1, SEQ, D), F32, kind="ExternalOutput").ap()
    build(nc, args, out)
    r = _run(nc, [arrays], core_ids=[0])
    return r.results[0]["out_0_dram"]
```
